# Optimizing a Trainium2 kernel written in Bass

```python
import jax, jax.numpy as jnp
from jax import lax
import numpy as np

D_MODEL = 1024
BATCH = 1
SEQ = 1024
DEPTH = 2

CONV_W = 512
CONV_K = 3
N_HEADS = 8
HEAD_DIM = 64
N_KV = 2
HPG = N_HEADS // N_KV
ATTN_W = N_HEADS * HEAD_DIM
KV_W = N_KV * HEAD_DIM
CMP_L = 32
CMP_D = 16
CMP_HIDDEN = 4 * HEAD_DIM
SEL_L = 64
N_SEL = 8
WINDOW = 512
Q_BLOCK = 128
FORCE_BONUS = 1e4
NEG = -1e30
D_FF = 4 * D_MODEL
ROPE_THETA = 10000.0
EPS = 1e-6
POS_OFFSET_MAX = 1024
IN_SIZES = (CONV_W, CONV_W, CONV_W, ATTN_W, KV_W, KV_W, KV_W, KV_W, KV_W, KV_W, 3 * N_HEADS, 2 * D_MODEL)
IN_W = sum(IN_SIZES)

kernel_name = "hybrid_conv_nsa_adaln_trunk"

def rmsnorm(x, g):
    xf = x.astype(jnp.float32)
    y = xf * lax.rsqrt(jnp.mean(xf * xf, axis=-1, keepdims=True) + EPS)
    return (y * g.astype(jnp.float32)).astype(x.dtype)

def rope_tables(positions):
    half = HEAD_DIM // 2
    inv_freq = ROPE_THETA ** (-jnp.arange(half, dtype=jnp.float32) * 2.0 / HEAD_DIM)
    ang = positions.astype(jnp.float32)[..., None] * inv_freq
    return jnp.cos(ang)[:, :, None, :], jnp.sin(ang)[:, :, None, :]

def apply_rope(x, cos, sin):
    half = HEAD_DIM // 2
    xf = x.astype(jnp.float32)
    x1, x2 = xf[..., :half], xf[..., half:]
    return jnp.concatenate([x1 * cos - x2 * sin, x2 * cos + x1 * sin], axis=-1).astype(x.dtype)

def masked_softmax(s, mask):
    s = jnp.where(mask, s.astype(jnp.float32), NEG)
    p = jax.nn.softmax(s, axis=-1)
    return jnp.where(mask, p, 0.0)

def short_conv_mixer(b_gate, c_gate, u, conv_w):
    v = c_gate * u
    w = conv_w.reshape(CONV_K, 1, CONV_W).astype(v.dtype)
    y = lax.conv_general_dilated(v, w, window_strides=(1,), padding=[(CONV_K - 1, 0)],
                                 dimension_numbers=('NWC', 'WIO', 'NWC'),
                                 feature_group_count=CONV_W)
    return b_gate * y

def compress_blocks(k, w1, w2, pe):
    B, S = k.shape[0], k.shape[1]
    nc = (S - CMP_L) // CMP_D + 1
    idx = np.arange(nc)[:, None] * CMP_D + np.arange(CMP_L)[None, :]
    blocks = jnp.swapaxes(k[:, idx], 2, 3) + pe
    flat = blocks.reshape(B, nc, N_KV, CMP_L * HEAD_DIM)
    return jax.nn.silu(flat @ w1) @ w2

def nsa_mixer(q, kc, vc, ks, vs, kw, vw, gate_logits, ck_w1, ck_w2, ck_pe, cv_w1, cv_w2, cv_pe):
    B, S = q.shape[0], q.shape[1]
    scale = HEAD_DIM ** -0.5
    qg = q.reshape(B, S, N_KV, HPG, HEAD_DIM)
    t = jnp.arange(S)

    kcmp = compress_blocks(kc, ck_w1, ck_w2, ck_pe)
    vcmp = compress_blocks(vc, cv_w1, cv_w2, cv_pe)
    nc = kcmp.shape[1]
    cstart = jnp.arange(nc) * CMP_D
    cmp_mask = (cstart + CMP_L - 1)[None, :] <= t[:, None]
    s_cmp = jnp.einsum('bsghd,bcgd->bsghc', qg, kcmp).astype(jnp.float32) * scale
    p_cmp = masked_softmax(s_cmp, cmp_mask[None, :, None, None, :])
    o_cmp = jnp.einsum('bsghc,bcgd->bsghd', p_cmp.astype(q.dtype), vcmp)

    ns = S // SEL_L
    j = jnp.arange(ns)
    overlap = ((cstart[:, None] < (j[None, :] + 1) * SEL_L) &
               (cstart[:, None] + CMP_L > j[None, :] * SEL_L)).astype(jnp.float32)
    imp = jnp.einsum('bsgc,cn->bsgn', p_cmp.sum(axis=3), overlap)
    blk_t = t // SEL_L
    valid = (j[None, :] <= blk_t[:, None])[:, None, :]
    forced = ((j[None, :] == 0) | (j[None, :] == blk_t[:, None]) | (j[None, :] == blk_t[:, None] - 1))[:, None, :]
    imp = jnp.where(valid, imp + FORCE_BONUS * forced.astype(jnp.float32), -1.0)
    n_sel = min(N_SEL, ns)
    _, sel_idx = lax.top_k(imp, n_sel)

    ks_blk = ks.reshape(B, ns, SEL_L, N_KV, HEAD_DIM).transpose(0, 3, 1, 2, 4)
    vs_blk = vs.reshape(B, ns, SEL_L, N_KV, HEAD_DIM).transpose(0, 3, 1, 2, 4)
    pad = ((0, 0), (WINDOW, 0), (0, 0), (0, 0))
    kw_pad = jnp.pad(kw, pad)
    vw_pad = jnp.pad(vw, pad)
    gather = jax.vmap(jax.vmap(lambda blk, ids: blk[ids]))

    def block_fn(qb):
        start = qb * Q_BLOCK
        q_b = lax.dynamic_slice_in_dim(qg, start, Q_BLOCK, 1)
        tq = start + jnp.arange(Q_BLOCK)
        ids = lax.dynamic_slice_in_dim(sel_idx, start, Q_BLOCK, 1).transpose(0, 2, 1, 3)
        ids_flat = ids.reshape(B, N_KV, Q_BLOCK * n_sel)
        k_sel = gather(ks_blk, ids_flat).reshape(B, N_KV, Q_BLOCK, n_sel * SEL_L, HEAD_DIM)
        v_sel = gather(vs_blk, ids_flat).reshape(B, N_KV, Q_BLOCK, n_sel * SEL_L, HEAD_DIM)
        kpos = (ids[..., None] * SEL_L + jnp.arange(SEL_L)).reshape(B, N_KV, Q_BLOCK, n_sel * SEL_L)
        m_sel = (kpos <= tq[None, None, :, None]).transpose(0, 2, 1, 3)[:, :, :, None, :]
        s_sel = jnp.einsum('bqghd,bgqkd->bqghk', q_b, k_sel).astype(jnp.float32) * scale
        p_sel = masked_softmax(s_sel, m_sel)
        o_sel = jnp.einsum('bqghk,bgqkd->bqghd', p_sel.astype(q.dtype), v_sel)
        k_w = lax.dynamic_slice_in_dim(kw_pad, start, Q_BLOCK + WINDOW, 1)
        v_w = lax.dynamic_slice_in_dim(vw_pad, start, Q_BLOCK + WINDOW, 1)
        kpos_w = start - WINDOW + jnp.arange(Q_BLOCK + WINDOW)
        m_w = ((kpos_w[None, :] <= tq[:, None]) & (kpos_w[None, :] > tq[:, None] - WINDOW)
               & (kpos_w[None, :] >= 0))
        s_w = jnp.einsum('bqghd,bkgd->bqghk', q_b, k_w).astype(jnp.float32) * scale
        p_w = masked_softmax(s_w, m_w[None, :, None, None, :])
        o_w = jnp.einsum('bqghk,bkgd->bqghd', p_w.astype(q.dtype), v_w)
        return o_sel, o_w

    o_sel, o_w = lax.map(block_fn, jnp.arange(S // Q_BLOCK))
    o_sel = jnp.swapaxes(o_sel, 0, 1).reshape(B, S, N_KV, HPG, HEAD_DIM)
    o_w = jnp.swapaxes(o_w, 0, 1).reshape(B, S, N_KV, HPG, HEAD_DIM)
    g = jax.nn.sigmoid(gate_logits).reshape(B, S, 3, N_KV, HPG)[..., None]
    o = g[:, :, 0] * o_cmp + g[:, :, 1] * o_sel + g[:, :, 2] * o_w
    return o.reshape(B, S, ATTN_W)

def setup_inputs(seed: int = 0) -> dict:
    key = jax.random.key(seed)
    ks = jax.random.split(key, 24)
    nrm = lambda k, shape, s: jax.random.normal(k, shape, jnp.float32) * s
    offs = jax.random.randint(ks[2], (BATCH, 1), 0, POS_OFFSET_MAX, dtype=jnp.int32)
    positions = (offs + jnp.arange(SEQ, dtype=jnp.int32)[None, :]).astype(jnp.int32)
    return {
        "x": nrm(ks[0], (BATCH, SEQ, D_MODEL), 1.0),
        "c": nrm(ks[1], (BATCH, D_MODEL), 1.0),
        "positions": positions,
        "w_ada": nrm(ks[3], (DEPTH, D_MODEL, 6 * D_MODEL), D_MODEL ** -0.5),
        "b_ada": nrm(ks[4], (DEPTH, 6 * D_MODEL), 0.01),
        "g_mix": 1.0 + nrm(ks[5], (DEPTH, D_MODEL), 0.02),
        "w_in": nrm(ks[6], (DEPTH, D_MODEL, IN_W), D_MODEL ** -0.5),
        "b_in": nrm(ks[7], (DEPTH, IN_W), 0.01),
        "conv_w": nrm(ks[8], (DEPTH, CONV_K, CONV_W), CONV_K ** -0.5),
        "cmp_k_w1": nrm(ks[9], (DEPTH, CMP_L * HEAD_DIM, CMP_HIDDEN), (CMP_L * HEAD_DIM) ** -0.5),
        "cmp_k_w2": nrm(ks[10], (DEPTH, CMP_HIDDEN, HEAD_DIM), CMP_HIDDEN ** -0.5),
        "cmp_k_pe": nrm(ks[11], (DEPTH, CMP_L, HEAD_DIM), 0.1),
        "cmp_v_w1": nrm(ks[12], (DEPTH, CMP_L * HEAD_DIM, CMP_HIDDEN), (CMP_L * HEAD_DIM) ** -0.5),
        "cmp_v_w2": nrm(ks[13], (DEPTH, CMP_HIDDEN, HEAD_DIM), CMP_HIDDEN ** -0.5),
        "cmp_v_pe": nrm(ks[14], (DEPTH, CMP_L, HEAD_DIM), 0.1),
        "w_up_conv": nrm(ks[15], (DEPTH, CONV_W, D_MODEL), CONV_W ** -0.5),
        "w_up_attn": nrm(ks[16], (DEPTH, ATTN_W, D_MODEL), ATTN_W ** -0.5),
        "w_o": nrm(ks[17], (DEPTH, D_MODEL, D_MODEL), D_MODEL ** -0.5),
        "g_mlp": 1.0 + nrm(ks[18], (DEPTH, D_MODEL), 0.02),
        "w_ff1": nrm(ks[19], (DEPTH, D_MODEL, D_FF), D_MODEL ** -0.5),
        "w_ff2": nrm(ks[20], (DEPTH, D_FF, D_MODEL), D_FF ** -0.5),
        "g_final": 1.0 + nrm(ks[21], (D_MODEL,), 0.02),
    }

def reference(x, c, positions, w_ada, b_ada, g_mix, w_in, b_in, conv_w, cmp_k_w1, cmp_k_w2, cmp_k_pe,
              cmp_v_w1, cmp_v_w2, cmp_v_pe, w_up_conv, w_up_attn, w_o, g_mlp, w_ff1, w_ff2, g_final):
    B, S, _ = x.shape
    cos, sin = rope_tables(positions)
    split_at = [int(v) for v in np.cumsum(IN_SIZES)[:-1]]
    c_act = jax.nn.silu(c)
    for l in range(DEPTH):
        cond = c_act @ w_ada[l] + b_ada[l]
        sh_a, sc_a, ga_a, sh_m, sc_m, ga_m = [v[:, None, :] for v in jnp.split(cond, 6, axis=-1)]

        h = rmsnorm(x, g_mix[l]) * (1.0 + sc_a) + sh_a
        z = h @ w_in[l] + b_in[l]
        (cb, cc, cu, q, kc, vc, k_s, v_s, k_w, v_w, nsa_g, merge_g) = jnp.split(z, split_at, axis=-1)
        y_conv = short_conv_mixer(cb, cc, cu, conv_w[l]) @ w_up_conv[l]
        q = apply_rope(q.reshape(B, S, N_HEADS, HEAD_DIM), cos, sin)
        kv = lambda a: a.reshape(B, S, N_KV, HEAD_DIM)
        kc = apply_rope(kv(kc), cos, sin)
        k_s = apply_rope(kv(k_s), cos, sin)
        k_w = apply_rope(kv(k_w), cos, sin)
        y_attn = nsa_mixer(q, kc, kv(vc), k_s, kv(v_s), k_w, kv(v_w), nsa_g,
                           cmp_k_w1[l], cmp_k_w2[l], cmp_k_pe[l],
                           cmp_v_w1[l], cmp_v_w2[l], cmp_v_pe[l]) @ w_up_attn[l]
        g_conv, g_attn = jnp.split(jax.nn.sigmoid(merge_g), 2, axis=-1)
        mixed = (g_conv * y_conv + g_attn * y_attn) @ w_o[l]
        x = x + ga_a * mixed

        h = rmsnorm(x, g_mlp[l]) * (1.0 + sc_m) + sh_m
        x = x + ga_m * (jnp.square(jax.nn.relu(h @ w_ff1[l])) @ w_ff2[l])
    return rmsnorm(x, g_final)


_drawn_inputs = setup_inputs


def setup_inputs(seed=0):
    import zlib

    import numpy as np

    out = dict(_drawn_inputs(seed))
    spreads = {}
    factors = {'b_in': 4.789, 'cmp_k_pe': 29.083, 'cmp_v_pe': 5.969, 'g_mlp': 2.786, 'g_final': 7.539}
    for name, (base, spread) in spreads.items():
        noise = np.random.default_rng([zlib.crc32(name.encode()), seed]).standard_normal(out[name].shape)
        drawn = base * np.exp(spread * noise) if base else spread * noise
        out[name] = __import__('jax').numpy.asarray(drawn.astype(out[name].dtype))
    for name, factor in factors.items():
        out[name] = (out[name] * factor).astype(out[name].dtype)
    return out
```

```python
from contextlib import ExitStack

import numpy as np

import concourse.bass as bass
from concourse import mybir

F32 = mybir.dt.float32
F32R = mybir.dt.float32r
BF16 = mybir.dt.bfloat16
I32 = mybir.dt.int32
ALU = mybir.AluOpType
ACT = mybir.ActivationFunctionType
AX = mybir.AxisListType

P = 128
DEPTH, SEQ, D = 2, 1024, 1024
KC = D // P
NT = SEQ // P
CONV_W, CONV_K = 512, 3
NH, HD, NKV = 8, 64, 2
HPG = NH // NKV
CMP_L, CMP_D, CMP_H = 32, 16, 256
NC = (SEQ - CMP_L) // CMP_D + 1
SEL_L, N_SEL = 64, 8
NS = SEQ // SEL_L
WIN_T = 512 // P
D_FF = 4 * D
FG = 4
NFG = D_FF // (FG * P)
NADA = 6 * KC
EPS = 1e-6
NEG = -1e30
BONUS = 1e4
TAKEN = 1e30
SCALE = HD ** -0.5
THETA = 10000.0

O_CB, O_CC, O_CU = 0, CONV_W, 2 * CONV_W
O_Q = 3 * CONV_W
O_KC, O_VC, O_KS, O_VS, O_KW, O_VW = (O_Q + NH * HD + i * NKV * HD for i in range(6))
O_NSA = O_VW + NKV * HD
NG = 3 * NH
O_MG = O_NSA + NG
IN_W = O_MG + 2 * D

R_ADA = 0
R_BIN = R_ADA + NADA
R_NSA = R_BIN + O_NSA // P
R_MG = R_NSA + 1
R_GMIX = R_MG + 2 * KC
R_GMLP = R_GMIX + KC
R_CONV = R_GMLP + KC
R_GFIN = R_CONV + CONV_K * CONV_W // P
R_END = R_GFIN + KC

RAW = 3
SPL = 2
ADA_FIRST = 2 * KC
CMP_T = 4
LPT = CMP_L // 2 // CMP_T


def weight_plan():
    tiles, chunk = [], {}
    ada = iter(range(ADA_FIRST, NADA))

    def dense(src, row, col, names, with_ada=False):
        for n in names:
            chunk[n] = len(chunk)
        tiles.append(("split", src, row, col, 8 // len(names), names))
        if with_ada:
            tiles.append(("ada", next(ada)))

    for j in range(CONV_W // P):
        for name, off in (("cc", O_CC), ("cu", O_CU), ("cb", O_CB)):
            dense("w_in", 0, off + P * j, [(name, j)], True)
    for i in range(0, KC, 2):
        dense("w_in", 0, O_MG + P * i, [("gc", i)], True)
        dense("w_in", 0, O_MG + P * (i + 1), [("gc", i + 1)], True)
        dense("w_up_conv", 0, P * i, [("uc", i), ("uc", i + 1)], True)
    for i in range(KC):
        dense("w_in", 0, O_MG + D + P * i, [("ga", i)], True)
    assert next(ada, None) is None
    for name, off in (("kc", O_KC), ("vc", O_VC), ("q0", O_Q), ("q1", O_Q + P)):
        dense("w_in", 0, off, [name])
    tiles += [("cmp", 0, t) for t in range(CMP_T)]
    dense("w_in", 0, O_Q + 2 * P, ["q2"])
    tiles += [("cmp", 1, t) for t in range(CMP_T)]
    for name, off in (("q3", O_Q + 3 * P), ("ks", O_KS), ("vs", O_VS), ("kw", O_KW), ("ns", O_NSA), ("vw", O_VW)):
        dense("w_in", 0, off, [name])
    for i in range(0, KC, 2):
        dense("w_up_attn", 0, P * i, [("ua", i), ("ua", i + 1)])
    for i in range(KC):
        dense("w_o", 0, P * i, [("wo", i)])

    def ff1(fg):
        for f in range(FG * fg, FG * fg + FG):
            dense("w_ff1", 0, P * f, [("f1", f)])
            if f < ADA_FIRST:
                tiles.append(("ada", f))

    ff1(0)
    for fg in range(NFG):
        if fg + 1 < NFG:
            ff1(fg + 1)
        for i in range(0, KC, 2):
            dense("w_ff2", FG * P * fg, P * i, [("f2", fg, i), ("f2", fg, i + 1)])
    return tiles, chunk


TILES, CHUNK = weight_plan()
IN_SLOT, SPLIT_NO, KIND_NO = [], {}, []
_count = [0] * RAW
for _n, _t in enumerate(TILES):
    _count[_n % RAW] += 32 if _t[0] == "cmp" else 16
    IN_SLOT.append(_count[_n % RAW])
    KIND_NO.append(sum(t[0] == _t[0] for t in TILES[:_n]))
    if _t[0] == "split":
        SPLIT_NO[_n] = KIND_NO[_n]
TILE_OF = {}
for _n, _t in enumerate(TILES):
    if _t[0] == "split":
        for _name in _t[5]:
            TILE_OF[_name] = _n
    else:
        TILE_OF[_t] = _n


def attention_plan():
    units, sets, flush = [("c", 0)], [], []
    for qt in range(NT):
        for g in range(NKV):
            for b in ("w", "s"):
                if b == "s" and g == NKV - 1 and qt + 1 < NT:
                    units.append(("c", qt + 1))
                lo = max(0, qt - WIN_T) if b == "w" else 0
                sets.append(dict(no=len(sets), b=b, qt=qt, g=g, lo=lo, n=(qt + 1 - lo) * P, first=len(units)))
                units += [(b, qt, g, i, len(sets) - 1) for i in range(HPG)]
                sets[-1]["last"] = len(units) - 1
    steps = [[] for _ in range(len(units) + T_AFTER + 3)]
    for s in sets:
        keys = list(range(s["lo"], s["qt"] + 1))
        e = s["last"]
        if s["b"] == "w" and s["g"] == 0:
            steps[e - 1].append(dict(kind="b", qt=s["qt"]))
        per = -(-len(keys) // 4)
        if s["b"] == "w":
            steps[e].append(dict(kind="c", qt=s["qt"], g=s["g"], first=True, last=False))
        for i, key in enumerate(keys):
            steps[e + T_AFTER + i // per].append(dict(kind="p", set=s, qt=s["qt"], g=s["g"], key=key, at=i * P, first=False,
                                                last=s["b"] == "s" and key == s["qt"], end=key == s["qt"]))
    groups = []
    for here in steps:
        for g in here:
            g.update(no=len(groups), bank=len(groups) % 2, v_no=sum(x["kind"] != "b" for x in groups))
            groups.append(g)
    waiting = []
    for u, here in enumerate(steps):
        for g in here:
            waiting += [g] * (g["kind"] != "b")
            g["then"] = [waiting.pop(0) for _ in range(len(waiting) - 2)]
        rest = []
        if not here or u == len(steps) - 1:
            rest, waiting = waiting, []
        flush.append(rest)
        for g in [v for x in here for v in x["then"]] + rest:
            if g["kind"] == "p" and g["last"]:
                g["set"]["fin"] = u + 1
    steps += [[], []]
    flush += [[], []]
    return units, sets, steps, flush, groups


SCALED_AFTER = (1, 2, 2, 3)
T_AFTER = 4
UNITS, SETS, STEPS, FLUSH, GROUPS = attention_plan()
SCORES_BEFORE = [sum(x[0] != "c" for x in UNITS[:u]) for u in range(len(UNITS) + 1)]
END_GROUP = {g["set"]["no"]: g for g in GROUPS if g["kind"] == "p" and g["end"]}
C_GROUP = {(g["qt"], g["g"]): g for g in GROUPS if g["kind"] == "c"}
B_GROUP = {g["qt"]: g for g in GROUPS if g["kind"] == "b"}
N_VGROUPS = sum(g["kind"] != "b" for g in GROUPS)
PROBS = 3
PT = 3
BRANCH = {"c": 0, "s": 1, "w": 2}


def trunk(nc, a, out):
    with ExitStack() as ctx:
        def sb(name, shape, dt=F32):
            return ctx.enter_context(nc.sbuf_tensor(name, shape, dt))

        def region(name, words, *layouts):
            found = []
            for layout in layouts:
                with ExitStack() as s:
                    found.append([s.enter_context(nc.sbuf_tensor(n, sh, dt)) for n, sh, dt in layout])
            sb(name, [P, words])
            return found

        every = []

        def sem(name):
            every.append(ctx.enter_context(nc.semaphore(name)))
            return every[-1]

        wraw = sb("wraw", [P, RAW, 1024])
        (whi, wlo), (prob3,) = region("r_w", 2 * SPL * 1024, [(n, [P, SPL, 1024], F32R) for n in ("whi", "wlo")],
                                      [("prob3", [P, HPG, SEQ], F32)])
        tmp = sb("tmp", [P, 2, SEQ])
        (xT,), (cosT, sinT, kcT, vcT, fbuf, ropes), (vw, vs, pTH, pTL, scm, psum4, negm, sums, cst, imp, top8, left, fac), (_, _, _, pTF) = region(
            "r_x", KC * SEQ, [("xT", [P, KC, SEQ], F32)],
            [("cosT", [P, SEQ], F32), ("sinT", [P, SEQ], F32), ("kcT", [P, SEQ], F32), ("vcT", [P, SEQ], F32),
             ("fbuf", [P, 2, SEQ], F32), ("ropes", [P, 2, SEQ], F32)],
            [("vw", [P, NT, NKV, P], F32R), ("vs", [P, NT, NKV, P], F32R), ("pTH", [P, PT, 512], F32R),
             ("pTL", [P, PT, 512], F32R), ("scm", [P, NH, 64], F32), ("psum4", [P, NKV, 65], F32),
             ("negm", [P, len(UNITS) - NT], F32), ("sums", [P, len(UNITS) - NT], F32), ("cst", [P, 3, NH], F32),
             ("imp", [P, NKV, NS], F32), ("top8", [P, NKV, 8], F32), ("left", [P, NKV, NS], F32),
             ("fac", [P, 2, HPG], F32)],
            [("vw_", [P, NT, NKV, P], F32R), ("vs_", [P, NT, NKV, P], F32R), ("pTH_", [P, PT, 512], F32R),
             ("pTF", [P, PT, 512], F32)])
        (hH, hL), (atH, atL, prob), (_, _, stG, stM), (xin,) = region(
            "r_h", 2 * KC * SEQ, [("hH", [P, KC, SEQ], F32R), ("hL", [P, KC, SEQ], F32R)],
            [("atH", [P, 4, SEQ], F32R), ("atL", [P, 4, SEQ], F32R), ("prob", [P, 2, HPG, SEQ], F32)],
            [("atH_", [P, 4, SEQ], F32R), ("atL_", [P, 4, SEQ], F32R), ("stG", [P, 2, SEQ], F32),
             ("stM", [P, 2, SEQ], F32)],
            [("xin", [P, NT, D], F32)])
        (qS, kwH, kwL, ksH, ksL), (_, blk, w2), (cvH, cvL), (mxH, mxL), (hidH, hidL), (nt, nf, pe_rows, crow), (outb,) = region(
            "r_m", 2 * KC * SEQ,
            [("qS", [P, NH, SEQ], F32R)] + [(n, [P, NKV, SEQ], F32R) for n in ("kwH", "kwL", "ksH", "ksL")],
            [("qS_", [P, NH, SEQ], F32R), ("blk", [P, CMP_L // 2, NKV * 64], F32), ("w2", [P, 2, 2, HD], F32)],
            [("cvH", [P, 4, SEQ], F32R), ("cvL", [P, 4, SEQ], F32R)],
            [("mxH", [P, KC, SEQ], F32R), ("mxL", [P, KC, SEQ], F32R)],
            [("hidH", [P, 2, FG, SEQ], F32R), ("hidL", [P, 2, FG, SEQ], F32R)],
            [("nt", [P, 2, SEQ], F32), ("nf", [P, 2, SEQ], F32), ("pe_rows", [CMP_L, 2 * P], F32),
             ("crow", [KC, P], F32)],
            [("outb", [P, NT, D], F32)])

        ident = sb("ident", [P, P])
        identb = sb("identb", [P, P], BF16)
        ones = sb("ones", [P, P])
        rot = sb("rot", [P, P])
        causal = sb("causal", [P, P], BF16)
        oldest = sb("oldest", [P, P], BF16)
        cmask = sb("cmask", [P, 120])
        vtab = sb("vtab", [P, 30])
        ftab = sb("ftab", [P, 30])
        rowok = sb("rowok", [P, 1])
        vecs = sb("vecs", [P, P])
        cols = sb("cols", [P, P])
        pe_cols = sb("pe_cols", [P, 2, CMP_L])
        adac = sb("adac", [P, NADA])
        modA = sb("modA", [P, 2, KC])
        qbias = sb("qbias", [P, 4])
        cT = sb("cT", [P, KC])
        csig = sb("csig", [P, KC])
        hsig, hsil = (tmp[:, 0, i * 256:i * 256 + 4 * NC].rearrange("p (i c) -> p i c", i=2) for i in range(2))
        low_half = tmp[0:HD, 0, 0:512]
        att = tmp[:, 0, 512:768]
        gates = tmp[:, 0, 768:768 + NT * NG].rearrange("p (t n) -> p t n", t=NT)
        selb = tmp[:, 0, 768 + NT * NG:SEQ].rearrange("p (g n) -> p g n", g=NKV)
        cprob, cgated = (tmp[:, 1, i * 512:(i + 1) * 512].rearrange("p (h c) -> p h c", h=NH) for i in range(2))
        kcmp = sb("kcmp", [P, NKV * NC])
        vcmp = sb("vcmp", [NC, NKV, P], F32R)
        blocks_of = sb("blocks_of", [P, SEQ], BF16)
        selT = sb("selT", [P, 2, NKV, P], BF16)
        adared = sb("adared", [P, 2, P])

        lin = [ctx.enter_context(nc.psum_tensor(f"lin{i}", [P, SEQ], F32)) for i in range(2)]
        aux = ctx.enter_context(nc.psum_tensor("aux", [P, SEQ], F32))
        pv = ctx.enter_context(nc.psum_tensor("pv", [P, 2, 512], F32))

        def prob_of(no, i):
            if no % PROBS < 2:
                return prob[:, no % PROBS, i, :]
            return prob3[:, i, :]

        x_keep = nc.dram_tensor("x_keep", [P, KC, SEQ], F32).ap()
        rope_keep = nc.dram_tensor("rope_keep", [2, P, SEQ], F32).ap()
        mix_keep = nc.dram_tensor("mix_keep", [KC, P, SEQ], F32).ap()
        gate_keep = nc.dram_tensor("gate_keep", [KC, P, SEQ], F32).ap()

        half = [slice(0, 512), slice(512, SEQ)]

        x_in, c_in, pos_in = sem("x_in"), sem("c_in"), sem("pos_in")
        tab_made, pool_step = sem("tab_made"), sem("pool_step")
        p_tr, p_ev = sem("p_tr"), sem("p_ev")
        p_small, p_vec, p_act = sem("p_small"), sem("p_vec"), sem("p_act")
        sq_made, ss_added = sem("sq_made"), sem("ss_added")
        rope_out, dve_p = sem("rope_out"), sem("dve_p")
        raw_in = [sem(f"raw_in{i}") for i in range(RAW)]
        ada_prod, ada_used, ada_mm = sem("ada_prod"), sem("ada_used"), sem("ada_mm")
        posr = tmp[0:1, 0, :]
        invr = vecs[0:1, :]

        def ada_tile(layer, j):
            return a["w_ada"][layer, :, P * j:P * (j + 1)].rearrange("(k p) n -> p k n", p=P)

        def ada_products(dve, n, no, arrived):
            w = wraw[:, n % RAW, :].rearrange("p (k n) -> p k n", k=KC)
            dve.wait_ge(raw_in[n % RAW], arrived)
            dve.tensor_tensor(w, w, cT[:, :].rearrange("p (k o) -> p k o", o=1).to_broadcast([P, KC, P]),
                              ALU.mult).then_inc(ada_prod, 1)
            dve.wait_ge(ada_prod, no + 1)
            if no >= 2:
                dve.wait_ge(ada_mm, no - 1)
            dve.tensor_reduce(adared[:, no % 2, :], w.rearrange("p k n -> p n k"), AX.X, ALU.add).then_inc(ada_used, 1)

        def ada_column(pe, out_col, no):
            pe.wait_ge(ada_used, no + 1)
            pe.matmul(out_col, adared[:, no % 2, :], ones[:, 0:1], start=True, stop=True).then_inc(ada_mm, 1)

        with nc.Block() as block:
            @block.sync
            def _(sp):
                sp.dma_start(crow[:, :], a["c"][0, :].rearrange("(k p) -> k p", p=P)).then_inc(c_in, 16)
                sp.dma_start(posr.bitcast(I32), a["positions"]).then_inc(pos_in, 16)
                for t in range(NT):
                    sp.dma_start(xin[:, t, :], a["x"][0, t * P:(t + 1) * P, :]).then_inc(x_in, 16)
                for j in range(ADA_FIRST):
                    if j >= RAW:
                        sp.wait_ge(ada_used, j - RAW + 1)
                    sp.dma_start(wraw[:, j % RAW, :].rearrange("p (k n) -> p k n", k=KC), ada_tile(0, j)).then_inc(raw_in[j % RAW], 16)
                sp.wait_ge(p_vec, 3)
                sp.dma_start(rope_keep[0], nt[:, 0, :]).then_inc(rope_out, 16)
                sp.wait_ge(p_act, 4)
                sp.dma_start(rope_keep[1], nt[:, 1, :]).then_inc(rope_out, 16)
                sp.wait_ge(rope_out, 32)

            @block.gpsimd
            def _(pool):
                n = [0]

                def then(ins):
                    n[0] += 1
                    ins.then_inc(pool_step, 1)
                    pool.wait_ge(pool_step, n[0])

                def keep(t, cond, pattern, base, cm, fill):
                    then(pool.affine_select(out=t, in_=t, pattern=pattern, compare_op=cond, fill=fill,
                                            base=base, channel_multiplier=cm))

                for t in (ident, identb):
                    then(pool.memset(t[:, :], 0.0))
                    keep(t[:, :], ALU.not_equal, [[-1, P]], 0, 1, 1.0)
                then(pool.memset(ones[:, :], 1.0))
                then(pool.memset(vecs[:, :], 0.0))
                for i in range(HD // 2):
                    f = float(np.float32(THETA) ** np.float32(-i * 2.0 / HD))
                    ins = pool.memset(invr.rearrange("o (r i) -> o r i", r=4)[:, :, i:i + 1], f)
                    then(ins)
                pool.sem_inc(tab_made, 1)
                then(pool.memset(rot[:, :], 0.0))
                rv = rot[:, :].rearrange("p (a i) -> p a i", a=2)
                keep(rv[:, :, 0:32], ALU.not_equal, [[-64, 2], [-1, 32]], -32, 1, -1.0)
                keep(rv[:, :, 32:64], ALU.not_equal, [[-64, 2], [-1, 32]], 0, 1, 1.0)
                then(pool.memset(causal[:, :], 0.0))
                keep(causal[:, :], ALU.is_ge, [[-1, P]], 0, 1, NEG)
                then(pool.memset(oldest[:, :], 0.0))
                keep(oldest[:, :], ALU.is_ge, [[1, P]], -1, -1, NEG)
                then(pool.memset(cmask[:, :], 0.0))
                keep(cmask[:, :], ALU.is_ge, [[-CMP_D, 120]], CMP_D * 56 - CMP_L + 1, 1, NEG)
                then(pool.memset(vtab[:, :], 1.0))
                keep(vtab[:, :], ALU.is_ge, [[-SEL_L, 30]], SEL_L * 14, 1, 0.0)
                then(pool.memset(ftab[:, :], BONUS))
                keep(ftab[:, :], ALU.is_ge, [[SEL_L, 30]], P - 1 - SEL_L * 14, -1, 0.0)
                keep(ftab[:, :], ALU.is_ge, [[-SEL_L, 30]], SEL_L * 14, 1, -1.0)
                then(pool.memset(rowok[:, :], 1.0))
                keep(rowok[:, :], ALU.is_ge, [[0, 1]], -(CMP_L - 1), 1, 0.0)
                then(pool.memset(selT[:, :, :, :], 0.0))
                then(pool.memset(blocks_of[:, :], 1.0))
                keep(blocks_of[:, :], ALU.is_ge, [[1, SEQ]], 0, -SEL_L, 0.0)
                keep(blocks_of[:, :], ALU.is_ge, [[-1, SEQ]], SEL_L - 1, SEL_L, 0.0)
                pool.wait_ge(p_small, 1)
                then(pool.memset(vecs[:, :], 0.0))

            @block.tensor
            def _(pe):
                pe.wait_ge(tab_made, 1)
                pe.wait_ge(c_in, 16)
                pe.transpose(pv[:, 0, 0:KC], crow[:, :], ident[0:KC, 0:KC])
                pe.matmul(pv[:, 0, 64:65], invr, ones[0:1, 0:1], start=True, stop=True).then_inc(p_small, 1)
                pe.wait_ge(p_vec, 1)
                for hf in half:
                    mm = pe.matmul(aux[:, hf], ones[0:1, :], tmp[0:1, 1, hf], start=True, stop=True)
                mm.then_inc(p_small, 1)
                for g in range(2 * KC):
                    k, hh = g // 2, g % 2
                    if g >= 4:
                        pe.wait_ge(p_ev, g - 3)
                    pe.wait_ge(x_in, 16 * NT)
                    for t in range(4):
                        tt = 4 * hh + t
                        mm = pe.transpose(lin[g // 2 % 2][:, g % 2 * 512 + t * P:g % 2 * 512 + (t + 1) * P],
                                          xin[:, tt, k * P:(k + 1) * P], ident[:, :])
                    mm.then_inc(p_tr, 1)
                for j in range(ADA_FIRST):
                    ada_column(pe, pv[:, 1, j:j + 1], j)

            @block.scalar
            def _(act):
                act.wait_ge(p_small, 1)
                act.activation(csig[:, :], pv[:, 0, 0:KC], ACT.Sigmoid).then_inc(p_act, 1)
                act.wait_ge(p_vec, 2)
                act.activation(nt[:, 1, :], nf[:, 0, :], ACT.Sin).then_inc(p_act, 1)
                act.activation(nf[:, 1, :], nf[:, 0, :], ACT.Sin, scale=0.5).then_inc(p_act, 1)
                act.wait_ge(p_act, 3)
                act.activation(nf[:, 0, :], nf[:, 1, :], ACT.Square).then_inc(p_act, 1)
                act.wait_ge(p_vec, 3)
                for k in range(KC):
                    act.wait_ge(p_ev, 2 * k + 2)
                    if k >= 2:
                        act.wait_ge(ss_added, k - 1)
                    act.activation(tmp[:, min(k, 1), :], xT[:, k, :], ACT.Square).then_inc(sq_made, 1)

            @block.vector
            def _(dve):
                n = [0]

                def then(ins):
                    n[0] += 1
                    ins.then_inc(dve_p, 1)
                    dve.wait_ge(dve_p, n[0])

                dve.wait_ge(pos_in, 16)
                dve.tensor_copy(tmp[0:1, 1, :], posr.bitcast(I32)).then_inc(p_vec, 1)
                dve.wait_ge(p_act, 1)
                dve.tensor_tensor(cT[:, :], csig[:, :], pv[:, 0, 0:KC], ALU.mult).then_inc(dve_p, 1)
                n[0] += 1
                inv = cols[:, 0:1]
                then(dve.tensor_copy(inv, pv[:, 0, 64:65]))
                dve.wait_ge(p_small, 2)
                ang, turns = nf[:, 0, :], nf[:, 1, :]
                then(dve.tensor_scalar(ang, aux[:, :], inv, None, ALU.mult))
                magic = 1.5 * 2.0 ** 23
                then(dve.tensor_scalar(turns, ang, 1.0 / (2 * np.pi), magic, ALU.mult, ALU.add))
                then(dve.tensor_scalar(turns, turns, magic, None, ALU.subtract))
                rest = 2 * np.pi
                for bits in (8, 8, 8, 24):
                    e = int(np.floor(np.log2(rest)))
                    part = float(np.float32(np.floor(rest / 2.0 ** (e - bits + 1)) * 2.0 ** (e - bits + 1)))
                    rest -= part
                    then(dve.scalar_tensor_tensor(out=ang, in0=turns, scalar=-part, in1=ang,
                                                  op0=ALU.mult, op1=ALU.add))
                pi = float(np.nextafter(np.float32(np.pi), np.float32(0)))
                dve.tensor_scalar(ang, ang, -pi, pi, ALU.max, ALU.min).then_inc(p_vec, 1)
                dve.wait_ge(p_act, 4)
                dve.tensor_scalar(nt[:, 0, :], nf[:, 0, :], -2.0, 1.0, ALU.mult, ALU.add).then_inc(p_vec, 1)
                for g in range(2 * KC):
                    k, hh = g // 2, g % 2
                    dve.wait_ge(p_tr, g + 1)
                    dve.tensor_copy(xT[:, k, half[hh]], lin[k % 2][:, half[hh]]).then_inc(p_ev, 1)
                    if g % 2 and k:
                        dve.wait_ge(sq_made, k + 1)
                        dve.tensor_tensor(tmp[:, 0, :], tmp[:, 0, :], tmp[:, 1, :], ALU.add).then_inc(ss_added, 1)
                        dve.wait_ge(ss_added, k)
                for j in range(ADA_FIRST):
                    ada_products(dve, j, j, 16 * (j // RAW + 1))
                dve.wait_ge(ada_mm, ADA_FIRST)
                dve.tensor_copy(adac[:, 0:ADA_FIRST], pv[:, 1, 0:ADA_FIRST]).then_inc(p_vec, 1)

        par_in, x_out, tab_in, dve_step = (sem(s) for s in ("par_in", "x_out", "tab_in", "dve_step"))
        mix_out, gate_out = ([sem(f"{n}{i}") for i in range(2)] for n in ("mix_out", "gate_out"))
        fetch_sem = [sem(f"fetch{i}") for i in range(2)]
        x_back = sem("x_back")
        w_hi, w_split, cmp_used = sem("w_hi"), sem("w_split"), sem("cmp_used")
        lin_done = sem("lin_done")
        lin_free = [sem(f"lin_free{i}") for i in range(2)]
        par_t, par_c, ss_done, ada_cols = (sem(s) for s in ("par_t", "par_c", "ss_done", "ada_cols"))
        ss_read, mean_made, root_made, rstd_made = (sem(s) for s in ("ss_read", "mean_made", "root_made", "rstd_made"))
        h_t, h_f, h_hi, h_lo = (sem(s) for s in ("h_t", "h_f", "h_hi", "h_lo"))
        cc_made, conv_made, cv_hi, cv_lo = (sem(s) for s in ("cc_made", "conv_made", "cv_hi", "cv_lo"))
        gc_made, mix_made, ga_made = (sem(s) for s in ("gc_made", "mix_made", "ga_made"))
        z_made, aux_done, aux_free, rope_made, blk_made = (sem(s) for s in ("z_made", "aux_done", "aux_free", "rope_made", "blk_made"))
        hid_sig, hid_silu, cmp_done, cmp_made = (sem(s) for s in ("hid_sig", "hid_silu", "cmp_done", "cmp_made"))
        rope_sum, rope_hi, v_hi, vc_lo = (sem(s) for s in ("rope_sum", "rope_hi", "v_hi", "vc_lo"))
        f_made, p_scaled = sem("f_made"), sem("p_scaled")
        t_hi, t_lo, fin_low, fin_sum, fin_lo = (sem(s) for s in ("t_hi", "t_lo", "fin_low", "fin_sum", "fin_lo"))
        s_done, max_made, exp_made = (sem(s) for s in ("s_done", "max_made", "exp_made"))
        c_in_made, c_exp, c_prob, sel_made = (sem(s) for s in ("c_in_made", "c_exp", "c_prob", "sel_made"))
        c_gated, t_done, v_done, o_hi = (sem(s) for s in ("c_gated", "t_done", "v_done", "o_hi"))
        t_free = [sem(f"t_free{i}") for i in range(2)]
        mg_read, mg_made, mg_hi, mg_lo = (sem(s) for s in ("mg_read", "mg_made", "mg_hi", "mg_lo"))
        x_made, relu_made, hid_sq, hid_hi, hid_lo = (sem(s) for s in ("x_made", "relu_made", "hid_sq", "hid_hi", "hid_lo"))

        def freed(eng, name):
            c = CHUNK[name]
            eng.wait_ge(lin_free[c % 2], c // 2 + 1)

        def done(eng, name):
            eng.wait_ge(lin_done, CHUNK[name] + 1)

        def slot(name):
            return lin[CHUNK[name] % 2]

        def free_sem(name):
            return lin_free[CHUNK[name] % 2]

        def col(r):
            return cols[:, r:r + 1]

        ROPED = ["kc", "q0", "q1", "q2", "q3", "ks", "kw"]
        Z = ["kc", "q0", "q1", "q2", "q3", "ks", "vs", "kw", "vw"]
        AUXED = ["kc", "q0", "q1", "q2", "q3", "ks", "vs", "kw", "nsaT", "vw"]
        NPAR = 8 + 4 + 2

        def clear():
            with nc.Block() as block:
                @block.sync
                def _(sp):
                    for s in every:
                        sp.sem_clear(s)

        clear()
        def chunks(s):
            if s["b"] == "w" and s["n"] == 5 * P:
                return [(0, 3 * P, P), (3 * P, 5 * P, 512)]
            return [(c, min(s["n"], c + 512), c) for c in range(0, s["n"], 512)]

        with nc.Fori(0, DEPTH) as layer:
            with nc.Block() as block:
                @block.sync
                def _(sp):
                    def source(t):
                        if t[0] == "split":
                            _, src, row, c0, k, _ = t
                            return a[src][layer, row:row + k * P, c0:c0 + 1024 // k].rearrange("(k p) n -> p k n", p=P)
                        return ada_tile(layer if t[1] >= ADA_FIRST else (layer + 1) % DEPTH, t[1])

                    for n, t in enumerate(TILES):
                        if n >= RAW:
                            o = n - RAW
                            sp.wait_ge(dict(split=w_split, ada=ada_used, cmp=cmp_used)[TILES[o][0]], KIND_NO[o] + 1)
                        ready = raw_in[n % RAW]
                        if t[0] == "cmp":
                            src = a["cmp_v_w1" if t[1] else "cmp_k_w1"]
                            for lh in range(2):
                                r0 = (lh * CMP_L // 2 + t[2] * LPT) * HD
                                sp.dma_start(wraw[64 * lh:64 * lh + 64, n % RAW, :].rearrange("p (k n) -> p k n", k=LPT),
                                             src[layer, r0:r0 + LPT * HD, :].rearrange("(k p) n -> p k n", p=HD)
                                             ).then_inc(ready, 16)
                        else:
                            k = t[4] if t[0] == "split" else KC
                            sp.dma_start(wraw[:, n % RAW, :].rearrange("p (k n) -> p k n", k=k), source(t)).then_inc(ready, 16)

                @block.gpsimd
                def _(pool):
                    def attention():
                        for u, here in enumerate(STEPS):
                            for st in SETS:
                                for i in range(HPG):
                                    if st["last"] + SCALED_AFTER[i] == u:
                                        pool.wait_ge(f_made, st["no"] + 1)
                                        p = prob_of(st["no"], i)[:, 0:st["n"]]
                                        pool.tensor_scalar(p, p, fac[:, st["no"] % 2, i:i + 1], 1.0, ALU.mult, ALU.mult).then_inc(p_scaled, 1)
                                        pool.wait_ge(p_scaled, HPG * st["no"] + i + 1)
                            for x in here:
                                if x["kind"] != "b":
                                    r, t = NC if x["kind"] == "c" else P, x["v_no"] % PT
                                    pool.wait_ge(t_free[x["bank"]], x["no"] // 2 + 1)
                                    pool.tensor_scalar(pTH[0:r, t, :], pTF[0:r, t, :], 1.0, 1.0, ALU.mult, ALU.mult).then_inc(t_hi, 1)
                                    pool.wait_ge(t_hi, x["v_no"] + 1)

                    for n, t in enumerate(TILES):
                        if t[0] != "split":
                            continue
                        s = SPLIT_NO[n]
                        if s:
                            pool.wait_ge(w_split, s)
                        if t[5][0] == ("ua", 0):
                            attention()
                            pool.wait_ge(t_done, END_GROUP[len(SETS) - 1]["no"] + 1)
                        pool.wait_ge(raw_in[n % RAW], IN_SLOT[n])
                        if s >= SPL:
                            before = [m for m in SPLIT_NO if SPLIT_NO[m] == s - SPL][0]
                            done(pool, TILES[before][5][-1])
                        pool.tensor_scalar(whi[:, s % SPL, :], wraw[:, n % RAW, :], 1.0, 1.0, ALU.mult, ALU.mult).then_inc(w_hi, 1)
                        pool.wait_ge(w_hi, s + 1)
                        pool.tensor_tensor(wlo[:, s % SPL, :], wraw[:, n % RAW, :], whi[:, s % SPL, :].bitcast(F32),
                                           ALU.subtract).then_inc(w_split, 1)

                @block.tensor
                def _(pe):
                    def dense(name, act_h, act_l, ready=None):
                        c, n = CHUNK[name], TILE_OF[name]
                        t, s = TILES[n], SPLIT_NO[n] % SPL
                        kk, j = t[4], t[5].index(name)
                        if j == 0:
                            pe.wait_ge(w_split, SPLIT_NO[n] + 1)
                        if c >= 2:
                            pe.wait_ge(lin_free[c % 2], c // 2)
                        for k in range(kk):
                            if ready:
                                ready(k)
                            at = k * (1024 // kk) + P * j
                            wh, wl = whi[:, s, at:at + P], wlo[:, s, at:at + P]
                            for w, m in ((wh, act_h), (wh, act_l), (wl, act_h)):
                                for hf in half:
                                    first = w is wh and m is act_h and k == 0
                                    last = w is wl and k == kk - 1
                                    mm = pe.matmul(lin[c % 2][:, hf], w, m(k)[:, hf], start=first, stop=last)
                        mm.then_inc(lin_done, 1)

                    ada_no, ada_late = [0], []

                    def ada(j):
                        if ada_late:
                            late = ada_late.pop()
                            ada_column(pe, pv[:, 0, late:late + 1], ada_no[0])
                            ada_no[0] += 1
                        if j is not None:
                            ada_late.append(j)

                    def sum_squares():
                        for hf in half:
                            mm = pe.matmul(aux[:, hf], ones[:, :], tmp[:, 0, hf], start=True, stop=True)
                        mm.then_inc(ss_done, 1)

                    def aux_begin(name):
                        i = AUXED.index(name)
                        if i:
                            pe.wait_ge(aux_free, i)

                    def rotate(name):
                        aux_begin(name)
                        pe.wait_ge(z_made, Z.index(name) + 1)
                        for hf in half:
                            mm = pe.matmul(aux[:, hf], rot[:, :], fbuf[:, Z.index(name) % 2, hf], start=True, stop=True)
                        mm.then_inc(aux_done, 1)

                    def token_major(name):
                        aux_begin(name)
                        pe.wait_ge(z_made, Z.index(name) + 1)
                        for t in range(NT):
                            mm = pe.transpose(aux[:, t * P:(t + 1) * P], fbuf[:, Z.index(name) % 2, t * P:(t + 1) * P], ident[:, :])
                        mm.then_inc(aux_done, 1)

                    def compress(kv):
                        pe.wait_ge(blk_made, kv + 1)
                        if kv:
                            pe.wait_ge(cmp_made, 2)
                        for t in range(CMP_T):
                            n = TILE_OF[("cmp", kv, t)]
                            pe.wait_ge(raw_in[n % RAW], IN_SLOT[n])
                            for i in range(LPT):
                                l = t * LPT + i
                                for hc in range(2):
                                    at = i * CMP_H + hc * P
                                    mm = pe.matmul(pv[:, hc, 0:2 * NC], wraw[:, n % RAW, at:at + P], blk[:, l, 0:2 * NC],
                                                   start=l == 0, stop=l == CMP_L // 2 - 1)
                            mm.then_inc(cmp_used, 1)

                    H = lambda k: hH[:, k, :]
                    L = lambda k: hL[:, k, :]

                    pe.wait_ge(par_in, 16 * NPAR)
                    pe.transpose(pv[:, 1, 0:P], vecs[:, :], ident[:, :])
                    for i in range(2):
                        mm = pe.transpose(pv[:, 1, P + 32 * i:P + 32 * i + 32], pe_rows[:, i * P:(i + 1) * P],
                                          ident[0:CMP_L, 0:CMP_L])
                    mm.then_inc(par_t, 1)
                    sum_squares()
                    nxt = iter(range(ADA_FIRST, NADA))
                    for j in range(CONV_W // P):
                        for name in ("cc", "cu", "cb"):
                            dense((name, j), H, L, (lambda k: pe.wait_ge(h_lo, k + 1)) if (name, j) == ("cc", 0) else None)
                            ada(next(nxt))
                    for i in range(0, KC, 2):
                        dense(("gc", i), H, L)
                        ada(next(nxt))
                        dense(("gc", i + 1), H, L)
                        ada(next(nxt))
                        if i == 0:
                            pe.wait_ge(cv_lo, 4)
                        dense(("uc", i), lambda k: cvH[:, k, :], lambda k: cvL[:, k, :])
                        dense(("uc", i + 1), lambda k: cvH[:, k, :], lambda k: cvL[:, k, :])
                        ada(next(nxt))
                    for i in range(KC):
                        dense(("ga", i), H, L)
                        ada(next(nxt))
                    dense("kc", H, L)
                    ada(None)
                    dense("vc", H, L)
                    rotate("kc")
                    dense("q0", H, L)
                    dense("q1", H, L)
                    rotate("q0")
                    pe.wait_ge(ada_cols, 2)
                    compress(0)
                    dense("q2", H, L)
                    rotate("q1")
                    pe.wait_ge(hid_silu, 1)
                    for hc in range(2):
                        mm = pe.matmul(pv[0:HD, 0, 256:256 + 2 * NC], w2[:, 0, hc, :], hsil[:, hc, :], start=hc == 0, stop=hc == 1)
                    mm.then_inc(cmp_done, 1)
                    compress(1)
                    dense("q3", H, L)
                    rotate("q2")
                    pe.wait_ge(hid_silu, 2)
                    for g in range(NKV):
                        for hc in range(2):
                            mm = pe.matmul(pv[0:NC, 0, 256 + g * HD:256 + (g + 1) * HD], hsil[:, hc, g * NC:(g + 1) * NC],
                                           w2[:, 1, hc, :], start=hc == 0, stop=hc == 1)
                    mm.then_inc(cmp_done, 1)
                    dense("ks", H, L)
                    rotate("q3")
                    dense("vs", H, L)
                    rotate("ks")
                    dense("kw", H, L)
                    token_major("vs")
                    rotate("kw")
                    dense("ns", H, L)
                    dense("vw", H, L)
                    aux_begin("nsaT")
                    freed(pe, "ns")
                    for t in range(NT):
                        mm = pe.transpose(aux[:, t * NG:(t + 1) * NG], tmp[0:NG, 1, t * P:(t + 1) * P], ident[0:NG, 0:NG])
                    mm.then_inc(aux_done, 1)
                    token_major("vw")

                    def score(u):
                        s = lin[u % 2]
                        if u >= 2:
                            if UNITS[u - 2][0] == "c":
                                pe.wait_ge(c_in_made, 1 + UNITS[u - 2][1])
                            else:
                                pe.wait_ge(exp_made, SCORES_BEFORE[u - 1])
                        b, qt = UNITS[u][:2]
                        qs = slice(qt * P, (qt + 1) * P)
                        if b == "c":
                            for h in range(NH):
                                mm = pe.matmul(s[:, h * P:h * P + NKV * NC], qS[:, h, qs].bitcast(F32), kcmp[:, :],
                                               start=h % HPG == 0, stop=h % HPG == HPG - 1, skip_group_check=True)
                            mm.then_inc(s_done, 1)
                            return
                        g, i, no = UNITS[u][2:]
                        st = SETS[no]
                        if b == "s" and i == 0 and g == 0:
                            b_ = B_GROUP[qt]
                            pe.wait_ge(t_free[b_["bank"]], b_["no"] // 2 + 1)
                        kh, kl = (kwH, kwL) if b == "w" else (ksH, ksL)
                        for c0, c1, at in chunks(st):
                            k0 = st["lo"] * P + c0
                            q = qS[:, HPG * g + i, qs]
                            wide = max(c1 - c0, 256)
                            mine = []
                            if b == "w" and qt >= WIN_T and c0 == 0:
                                mine.append((at, oldest))
                            if c1 == st["n"]:
                                mine.append((at + c1 - c0 - P, causal))
                            pe.matmul(s[:, at:at + wide], q, kh[:, g, k0:k0 + wide], start=True, stop=False)
                            mm = pe.matmul(s[:, at:at + wide], q, kl[:, g, k0:k0 + wide], start=False, stop=b == "w" and not mine)
                            if b == "s":
                                mm = pe.matmul(s[:, at:at + wide], selT[:, qt % 2, g, :], blocks_of[:, k0:k0 + wide],
                                               start=False, stop=not mine)
                            for j, (m0, m) in enumerate(mine):
                                mm = pe.matmul(s[:, m0:m0 + P], identb[:, :], m[:, :], start=False, stop=j == len(mine) - 1)
                        mm.then_inc(s_done, 1)

                    def transpose_group(x):
                        if x["no"] >= 2:
                            pe.wait_ge(t_free[x["bank"]], x["no"] // 2)
                        o = aux[:, x["bank"] * 512:(x["bank"] + 1) * 512]
                        if x["kind"] == "b":
                            pe.wait_ge(sel_made, x["qt"] + 1)
                            mm = pe.transpose(o[0:64, 0:P], selb[:, :, :].rearrange("p g n -> p (g n)"), ident[:, :])
                        elif x["kind"] == "c":
                            pe.wait_ge(c_gated, x["qt"] + 1)
                            for i in range(HPG):
                                mm = pe.transpose(o[0:NC, i * P:(i + 1) * P], cgated[:, HPG * x["g"] + i, 0:NC], ident[:, :])
                        else:
                            no = x["set"]["no"]
                            pe.wait_ge(p_scaled, HPG * (no + 1))
                            for i in range(HPG):
                                mm = pe.transpose(o[:, i * P:(i + 1) * P], prob_of(no, i)[:, x["at"]:x["at"] + P], ident[:, :])
                        mm.then_inc(t_done, 1)

                    def values(x):
                        if x["first"] and x["qt"]:
                            pe.wait_ge(fin_sum, 2 * (NKV * (x["qt"] - 1) + x["g"] + 1))
                        pe.wait_ge(t_lo, x["v_no"] + 1)
                        r = NC if x["kind"] == "c" else P
                        if x["kind"] == "c":
                            v = vcmp[:, x["g"], :]
                        else:
                            v = (vw if x["set"]["b"] == "w" else vs)[:, x["key"], x["g"], :]
                        pe.matmul(pv[:, x["g"], :], v, pTH[0:r, x["v_no"] % PT, :], start=x["first"], stop=False)
                        pe.matmul(pv[:, x["g"], :], v, pTL[0:r, x["v_no"] % PT, :], start=False, stop=x["last"]).then_inc(v_done, 1)

                    pe.wait_ge(aux_free, len(AUXED))
                    pe.wait_ge(rope_made, len(ROPED))
                    pe.wait_ge(cmp_made, 3)
                    pe.wait_ge(vc_lo, 1)
                    freed(pe, "kw")
                    freed(pe, "vw")
                    score(0)
                    for u, here in enumerate(STEPS):
                        if u + 1 < len(UNITS):
                            score(u + 1)
                        for x in here:
                            transpose_group(x)
                            for v in x["then"]:
                                values(v)
                        for v in FLUSH[u]:
                            values(v)

                    pe.wait_ge(exp_made, SCORES_BEFORE[-1])
                    pe.wait_ge(fin_lo, NKV * NT)
                    for i in range(KC):
                        dense(("ua", i), lambda k: atH[:, k, :], lambda k: atL[:, k, :])
                    for i in range(KC):
                        dense(("wo", i), lambda k: mxH[:, k, :], lambda k: mxL[:, k, :],
                              (lambda k: pe.wait_ge(mg_lo, k + 1)) if i == 0 else None)
                    pe.wait_ge(ss_added, KC - 1)
                    sum_squares()

                    def ff1(fg):
                        for f in range(FG * fg, FG * fg + FG):
                            dense(("f1", f), H, L, (lambda k: pe.wait_ge(h_lo, KC + k + 1)) if f == 0 else None)
                            if f < ADA_FIRST:
                                ada(f)
                            elif f == ADA_FIRST:
                                ada(None)

                    ff1(0)
                    for fg in range(NFG):
                        if fg + 1 < NFG:
                            ff1(fg + 1)
                        pe.wait_ge(hid_lo, FG * (fg + 1))
                        for i in range(KC):
                            dense(("f2", fg, i), lambda k: hidH[:, fg % 2, k, :], lambda k: hidL[:, fg % 2, k, :])

                @block.scalar
                def _(act):
                    def rows(r, n, src):
                        act.dma_start(vecs[r:r + n, :], src).then_inc(par_in, 16)

                    rows(R_ADA, NADA, a["b_ada"][layer, :].rearrange("(r p) -> r p", p=P))
                    rows(R_BIN, O_NSA // P, a["b_in"][layer, 0:O_NSA].rearrange("(r p) -> r p", p=P))
                    act.dma_start(vecs[R_NSA:R_NSA + 1, 0:NG], a["b_in"][layer, O_NSA:O_MG].rearrange("(r p) -> r p", p=NG)
                                  ).then_inc(par_in, 16)
                    rows(R_MG, 2 * KC, a["b_in"][layer, O_MG:IN_W].rearrange("(r p) -> r p", p=P))
                    rows(R_GMIX, KC, a["g_mix"][layer, :].rearrange("(r p) -> r p", p=P))
                    rows(R_GMLP, KC, a["g_mlp"][layer, :].rearrange("(r p) -> r p", p=P))
                    rows(R_CONV, CONV_K * CONV_W // P, a["conv_w"][layer, :, :].rearrange("k (j p) -> (k j) p", p=P))
                    rows(R_GFIN, KC, a["g_final"].rearrange("(r p) -> r p", p=P))
                    for i, name in enumerate(("cmp_k_pe", "cmp_v_pe")):
                        for j in range(2):
                            act.dma_start(pe_rows[:, i * P + j * HD:i * P + (j + 1) * HD], a[name][layer, :, :]).then_inc(par_in, 16)
                    for i, name in enumerate(("cmp_k_w2", "cmp_v_w2")):
                        act.dma_start(w2[:, i, :, :], a[name][layer, :, :].rearrange("(k p) n -> p k n", p=P)).then_inc(par_in, 16)
                    act.dma_start(x_keep, xT[:, :, :]).then_inc(x_out, 16)

                    def norm(n):
                        act.wait_ge(mean_made, n + 1)
                        act.activation(tmp[:, 1, :], tmp[:, 0, :], ACT.Sqrt).then_inc(root_made, 1)
                        act.wait_ge(ada_cols, 3 if n else 1)
                        for k in range(KC):
                            m = n * KC + k
                            act.wait_ge(h_t, m + 1)
                            if k >= 2:
                                act.wait_ge(h_lo, m - 1)
                            sh = adac[:, 3 * n * KC + k:3 * n * KC + k + 1]
                            act.activation(nf[:, k % 2, :], nt[:, k % 2, :], ACT.Identity, bias=sh,
                                           scale=modA[:, n, k:k + 1]).then_inc(h_f, 1)
                            act.wait_ge(h_f, m + 1)
                            act.activation(hH[:, k, :], nf[:, k % 2, :], ACT.Copy).then_inc(h_hi, 1)

                    norm(0)
                    act.wait_ge(x_out, 16)
                    act.wait_ge(h_t, KC)
                    for i, t in enumerate((cosT, sinT)):
                        act.dma_start(t[:, :], rope_keep[i]).then_inc(tab_in, 16)
                    for j in range(CONV_W // P):
                        if j:
                            freed(act, ("cu", j - 1))
                        done(act, ("cc", j))
                        act.activation(fbuf[:, 0, :], slot(("cc", j))[:, :], ACT.Identity,
                                       bias=col(R_BIN + O_CC // P + j)).then_inc(free_sem(("cc", j)), 1)
                        act.wait_ge(conv_made, j + 1)
                        act.activation(cvH[:, j, :], ropes[:, 1, :], ACT.Copy).then_inc(cv_hi, 1)
                    for i in range(0, KC, 2):
                        for ii in (i, i + 1):
                            if ii >= 2:
                                freed(act, ("uc", ii - 2))
                            else:
                                act.wait_ge(cv_lo, CONV_W // P)
                            done(act, ("gc", ii))
                            act.activation(fbuf[:, ii % 2, :], slot(("gc", ii))[:, :], ACT.Sigmoid,
                                           bias=col(R_MG + ii)).then_inc(free_sem(("gc", ii)), 1)
                        for ii in (i, i + 1):
                            freed(act, ("uc", ii))
                            act.dma_start(mix_keep[ii], tmp[:, ii % 2, :]).then_inc(mix_out[ii % 2], 16)
                    for i in range(KC):
                        if i >= 2:
                            act.wait_ge(gate_out[i % 2], 16 * (i // 2))
                        done(act, ("ga", i))
                        act.activation(ropes[:, i % 2, :], slot(("ga", i))[:, :], ACT.Sigmoid,
                                       bias=col(R_MG + KC + i)).then_inc(free_sem(("ga", i)), 1)
                        freed(act, ("ga", i))
                        act.dma_start(gate_keep[i], ropes[:, i % 2, :]).then_inc(gate_out[i % 2], 16)
                    for i in range(2):
                        act.wait_ge(mix_out[i], 8 * KC)
                        act.wait_ge(gate_out[i], 8 * KC)

                    def z(name, row, bias=None, scale=1.0):
                        i = Z.index(name)
                        if i >= 2:
                            o = Z[i - 2]
                            if o in ROPED:
                                act.wait_ge(rope_made, ROPED.index(o) + 1)
                            else:
                                act.wait_ge(aux_done, AUXED.index(o) + 1)
                        done(act, name)
                        act.activation(fbuf[:, i % 2, :], slot(name)[:, :], ACT.Identity,
                                       bias=col(row) if bias is None else bias, scale=scale).then_inc(z_made, 1)
                        act.wait_ge(z_made, i + 1)
                        act.sem_inc(free_sem(name), 1)

                    def q(j):
                        z(f"q{j}", 0, qbias[:, j:j + 1], SCALE)

                    def silu(kv):
                        act.wait_ge(cmp_used, CMP_T * (kv + 1))
                        act.activation(hsig[:, :, :], pv[:, :, 0:2 * NC], ACT.Sigmoid).then_inc(hid_sig, 1)

                    def rope_high(name):
                        i = ROPED.index(name)
                        act.wait_ge(rope_sum, i + 1)
                        for g in range(2):
                            rows = slice(HD * g, HD * (g + 1))
                            t = ropes[rows, 0, :]
                            if name[0] == "q":
                                act.activation(qS[rows, 2 * int(name[1]) + g, :], t, ACT.Copy).then_inc(rope_hi, 1)
                            else:
                                kh = ksH if name == "ks" else kwH
                                for r in range(2):
                                    act.activation(kh[HD * r:HD * (r + 1), g, :], t, ACT.Copy).then_inc(rope_hi, 1)

                    def v_high(name, v):
                        act.wait_ge(aux_done, AUXED.index(name) + 1)
                        act.activation(v[:, :, :, 0:HD], aux[:, :].rearrange("p (t g d) -> p t g d", t=NT, g=NKV),
                                       ACT.Copy).then_inc(v_hi, 1)

                    B = lambda o: R_BIN + o // P
                    z("kc", B(O_KC))
                    done(act, "vc")
                    act.activation(vcT[:, :], slot("vc")[:, :], ACT.Identity, bias=col(B(O_VC))).then_inc(free_sem("vc"), 1)
                    q(0)
                    q(1)
                    rope_high("q0")
                    silu(0)
                    q(2)
                    rope_high("q1")
                    act.wait_ge(cmp_done, 1)
                    for r in range(2):
                        act.activation(kcmp[HD * r:HD * (r + 1), :], pv[0:HD, 0, 256:256 + 2 * NC], ACT.Copy).then_inc(cmp_made, 1)
                    silu(1)
                    q(3)
                    rope_high("q2")
                    act.wait_ge(cmp_done, 2)
                    act.activation(vcmp[:, :, 0:HD], pv[0:NC, 0, 256:256 + 2 * HD].rearrange("p (g c) -> p g c", g=NKV),
                                   ACT.Copy).then_inc(cmp_made, 1)
                    z("ks", B(O_KS))
                    rope_high("q3")
                    z("vs", B(O_VS))
                    rope_high("ks")
                    z("kw", B(O_KW))
                    act.wait_ge(blk_made, 2)
                    v_high("vs", vs)
                    done(act, "ns")
                    act.activation(tmp[0:NG, 1, :], slot("ns")[0:NG, :], ACT.Sigmoid, bias=cols[0:NG, R_NSA:R_NSA + 1]
                                   ).then_inc(free_sem("ns"), 1)
                    rope_high("kw")
                    z("vw", B(O_VW))
                    act.wait_ge(rope_sum, len(ROPED))
                    v_high("vw", vw)

                    act.wait_ge(aux_free, len(AUXED))
                    for u, here in enumerate(STEPS):
                        if u < len(UNITS) and UNITS[u][0] == "c":
                            qt = UNITS[u][1]
                            act.wait_ge(c_in_made, qt + 1)
                            if qt:
                                act.wait_ge(c_gated, qt)
                            act.activation(cprob[:, :, 0:NC], scm[:, :, 0:NC], ACT.Exp).then_inc(c_exp, 1)
                        elif u < len(UNITS):
                            b, qt, g, i, no = UNITS[u]
                            m, st = SCORES_BEFORE[u], SETS[no]
                            if no >= PROBS and i == 0:
                                act.wait_ge(t_done, END_GROUP[no - PROBS]["no"] + 1)
                            act.wait_ge(max_made, m + 1)
                            at = chunks(st)[0][2]
                            act.activation(prob_of(no, i)[:, 0:st["n"]], lin[u % 2][:, at:at + st["n"]], ACT.Exp,
                                           bias=negm[:, m:m + 1], accum_out=sums[:, m:m + 1]).then_inc(exp_made, 1)
                        for x in here:
                            o = aux[:, x["bank"] * 512:(x["bank"] + 1) * 512]
                            act.wait_ge(t_done, x["no"] + 1)
                            if x["kind"] == "b":
                                if x["qt"] >= 2:
                                    act.wait_ge(s_done, [s for s in SETS if s["qt"] == x["qt"] - 2][-1]["last"] + 1)
                                for g in range(NKV):
                                    ins = act.activation(selT[0:NS, x["qt"] % 2, g, :], o[32 * g:32 * g + NS, 0:P], ACT.Copy)
                                ins.then_inc(t_free[x["bank"]], 1)
                            else:
                                r = NC if x["kind"] == "c" else P
                                if x["v_no"] >= PT:
                                    act.wait_ge(v_done, x["v_no"] - PT + 1)
                                act.activation(pTF[0:r, x["v_no"] % PT, :], o[0:r, :], ACT.Copy).then_inc(t_free[x["bank"]], 1)
                        for st in SETS:
                            if st["b"] != "s":
                                continue
                            k = NKV * st["qt"] + st["g"]
                            if st["fin"] == u:
                                act.wait_ge(v_done, END_GROUP[st["no"]]["v_no"] + 1)
                                if k:
                                    act.wait_ge(fin_sum, 2 * k)
                                act.activation(low_half, pv[HD:P, st["g"], :], ACT.Copy).then_inc(fin_low, 1)
                            if st["fin"] + 1 == u:
                                act.wait_ge(fin_sum, 2 * (k + 1))
                                act.activation(atH[:, 2 * st["g"]:2 * st["g"] + 2, st["qt"] * P:(st["qt"] + 1) * P],
                                               att.rearrange("p (j t) -> p j t", j=2), ACT.Copy).then_inc(o_hi, 1)

                    act.wait_ge(v_done, N_VGROUPS)
                    act.wait_ge(fin_lo, NKV * NT)
                    act.dma_start(xT[:, :, :], x_keep).then_inc(x_back, 16)
                    for i in range(KC + 2):
                        if i < KC:
                            if i >= 2:
                                act.wait_ge(mg_made, i - 1)
                            act.dma_start(stG[:, i % 2, :], gate_keep[i]).then_inc(fetch_sem[i % 2], 16)
                            act.dma_start(stM[:, i % 2, :], mix_keep[i]).then_inc(fetch_sem[i % 2], 16)
                        if i >= 2:
                            act.wait_ge(mg_made, i - 1)
                            act.activation(mxH[:, i - 2, :], tmp[:, i % 2, :], ACT.Copy).then_inc(mg_hi, 1)

                    def squares(i, n):
                        act.wait_ge(x_made, (NFG - 1) * KC * n + n * KC + i + 1)
                        if i >= 2:
                            act.wait_ge(ss_added, n * (KC - 1) + i - 1)
                        act.activation(tmp[:, min(i, 1), :], xT[:, i, :], ACT.Square).then_inc(sq_made, 1)

                    act.wait_ge(mg_lo, KC)
                    for i in range(KC):
                        squares(i, 0)
                    norm(1)

                    def ff1(fg):
                        for f in range(FG * fg, FG * fg + FG):
                            done(act, ("f1", f))
                            if f:
                                act.wait_ge(hid_sq, f)
                                act.wait_ge(hid_hi, f)
                            else:
                                act.wait_ge(h_lo, 2 * KC)
                            act.activation(tmp[:, 0, :], slot(("f1", f))[:, :], ACT.Relu).then_inc(relu_made, 1)
                            act.wait_ge(relu_made, f + 1)
                            act.sem_inc(free_sem(("f1", f)), 1)
                            if fg >= 2:
                                done(act, ("f2", fg - 2, KC - 1))
                            act.activation(hidH[:, fg % 2, f % FG, :], tmp[:, 0, :], ACT.Square).then_inc(hid_hi, 1)

                    for fg in range(NFG):
                        ff1(fg)
                    act.wait_ge(hid_lo, NFG * FG)
                    for i in range(KC):
                        squares(i, 1)

                @block.vector
                def _(dve):
                    n_then = [0]

                    def then(ins):
                        n_then[0] += 1
                        ins.then_inc(dve_step, 1)
                        dve.wait_ge(dve_step, n_then[0])

                    dve.wait_ge(par_t, 1)
                    dve.tensor_copy(pe_cols[:, :, :].rearrange("p i l -> p (i l)"), pv[:, 1, P:P + 2 * CMP_L]).then_inc(par_c, 1)
                    then(dve.tensor_copy(cols[:, :], pv[:, 1, 0:P]))
                    qr = R_BIN + O_Q // P
                    then(dve.tensor_scalar(qbias[:, :], cols[:, qr:qr + 4], SCALE, None, ALU.mult))

                    def mod(n):
                        sc = adac[:, (3 * n + 1) * KC:(3 * n + 2) * KC]
                        g = cols[:, (R_GMLP if n else R_GMIX):(R_GMLP if n else R_GMIX) + KC]
                        return dve.scalar_tensor_tensor(out=modA[:, n, :], in0=sc, scalar=1.0, in1=g, op0=ALU.add, op1=ALU.mult)

                    def ada_part(lo, hi):
                        then(dve.tensor_tensor(adac[:, lo:hi], pv[:, 0, lo:hi], cols[:, R_ADA + lo:R_ADA + hi], ALU.add))

                    ada_tiles = iter([n for n, t in enumerate(TILES) if t[0] == "ada"])

                    def ada():
                        n = next(ada_tiles)
                        ada_products(dve, n, KIND_NO[n], IN_SLOT[n])

                    def norm(n):
                        dve.wait_ge(ss_done, n + 1)
                        dve.tensor_scalar(tmp[:, 0, :], aux[:, :], 1.0 / D, EPS, ALU.mult, ALU.add).then_inc(mean_made, 1)
                        dve.wait_ge(root_made, n + 1)
                        dve.reciprocal(tmp[:, 0, :], tmp[:, 1, :]).then_inc(rstd_made, 1)
                        dve.wait_ge(rstd_made, n + 1)
                        if n == 0:
                            then(dve.tensor_tensor(adac[:, 0:ADA_FIRST], adac[:, 0:ADA_FIRST], cols[:, R_ADA:R_ADA + ADA_FIRST], ALU.add))
                            mod(0).then_inc(ada_cols, 1)

                        def low(k):
                            m = n * KC + k
                            dve.wait_ge(h_hi, m + 1)
                            dve.tensor_tensor(hL[:, k, :], nf[:, k % 2, :], hH[:, k, :].bitcast(F32), ALU.subtract).then_inc(h_lo, 1)

                        for k in range(KC):
                            m = n * KC + k
                            if k >= 2:
                                dve.wait_ge(h_f, m - 1)
                            dve.tensor_tensor(nt[:, k % 2, :], xT[:, k, :], tmp[:, 0, :], ALU.mult).then_inc(h_t, 1)
                            if k:
                                low(k - 1)
                        low(KC - 1)

                    norm(0)
                    v, y, cf = fbuf[:, 1, :], ropes[:, 0, :], ropes[:, 1, :]
                    dve.wait_ge(x_out, 16)
                    for j in range(CONV_W // P):
                        ada()
                        freed(dve, ("cc", j))
                        done(dve, ("cu", j))
                        dve.scalar_tensor_tensor(out=v, in0=slot(("cu", j))[:, :], scalar=col(R_BIN + O_CU // P + j), in1=fbuf[:, 0, :],
                                                 op0=ALU.add, op1=ALU.mult).then_inc(free_sem(("cu", j)), 1)
                        freed(dve, ("cu", j))
                        w = [col(R_CONV + k * (CONV_W // P) + j) for k in range(CONV_K)]
                        then(dve.tensor_scalar(y, v, w[2], None, ALU.mult))
                        then(dve.scalar_tensor_tensor(out=y[:, 1:SEQ], in0=v[:, 0:SEQ - 1], scalar=w[1], in1=y[:, 1:SEQ], op0=ALU.mult, op1=ALU.add))
                        then(dve.scalar_tensor_tensor(out=y[:, 2:SEQ], in0=v[:, 0:SEQ - 2], scalar=w[0], in1=y[:, 2:SEQ], op0=ALU.mult, op1=ALU.add))
                        ada()
                        done(dve, ("cb", j))
                        dve.scalar_tensor_tensor(out=cf, in0=slot(("cb", j))[:, :], scalar=col(R_BIN + O_CB // P + j), in1=y,
                                                 op0=ALU.add, op1=ALU.mult).then_inc(conv_made, 1)
                        dve.wait_ge(conv_made, j + 1)
                        dve.sem_inc(free_sem(("cb", j)), 1)
                        dve.wait_ge(cv_hi, j + 1)
                        dve.tensor_tensor(cvL[:, j, :], cf, cvH[:, j, :].bitcast(F32), ALU.subtract).then_inc(cv_lo, 1)
                        ada()
                    dve.wait_ge(h_lo, KC)
                    for i in range(KC):
                        if i % 2 == 0:
                            ada()
                            ada()
                        freed(dve, ("gc", i))
                        done(dve, ("uc", i))
                        if i >= 2:
                            dve.wait_ge(mix_out[i % 2], 16 * (i // 2))
                        dve.tensor_tensor(tmp[:, i % 2, :], slot(("uc", i))[:, :], fbuf[:, i % 2, :], ALU.mult).then_inc(free_sem(("uc", i)), 1)
                        if i % 2:
                            ada()
                    for i in range(KC):
                        ada()
                    dve.wait_ge(ada_mm, NADA - ADA_FIRST)
                    ada_part(ADA_FIRST, NADA)
                    dve.sem_inc(ada_cols, 1)
                    mod(1).then_inc(ada_cols, 1)

                    def rope(name):
                        i = ROPED.index(name)
                        f, t1, t2 = fbuf[:, Z.index(name) % 2, :], ropes[:, 0, :], ropes[:, 1, :]
                        dve.wait_ge(z_made, Z.index(name) + 1)
                        if i:
                            dve.wait_ge(rope_made, i)
                        dve.tensor_tensor(t2, f, cosT[:, :], ALU.mult).then_inc(dve_step, 1)
                        n_then[0] += 1
                        dve.wait_ge(aux_done, AUXED.index(name) + 1)
                        dve.tensor_tensor(t1, aux[:, :], sinT[:, :], ALU.mult).then_inc(aux_free, 1)
                        dve.wait_ge(aux_free, AUXED.index(name) + 1)
                        dve.wait_ge(dve_step, n_then[0])
                        if name == "kc":
                            dve.tensor_tensor(kcT[:, :], t1, t2, ALU.add).then_inc(rope_made, 1)
                            dve.sem_inc(rope_sum, 1)
                            return
                        dve.tensor_tensor(t1, t1, t2, ALU.add).then_inc(rope_sum, 1)
                        dve.wait_ge(rope_sum, i + 1)
                        dve.wait_ge(rope_hi, 2 * min(i, 4) + 4 * max(0, i - 4))
                        for g in range(2):
                            rows = slice(HD * g, HD * (g + 1))
                            if name[0] == "q":
                                h = 2 * int(name[1]) + g
                                ins = dve.tensor_tensor(qS[HD * (1 - g):HD * (2 - g), h, :], t1[rows], qS[rows, h, :].bitcast(F32), ALU.subtract)
                            else:
                                kh, kl = (ksH, ksL) if name == "ks" else (kwH, kwL)
                                for r in range(2):
                                    ins = dve.tensor_tensor(kl[HD * r:HD * (r + 1), g, :], t1[rows], kh[rows, g, :].bitcast(F32), ALU.subtract)
                        ins.then_inc(rope_made, 1)

                    def v_low(name, v):
                        dve.wait_ge(v_hi, 1 + (name == "vw"))
                        dve.tensor_tensor(v[:, :, :, HD:P], aux[:, :].rearrange("p (t g d) -> p t g d", t=NT, g=NKV),
                                          v[:, :, :, 0:HD].bitcast(F32), ALU.subtract).then_inc(aux_free, 1)

                    def blocks(kv):
                        src = vcT if kv else kcT
                        for g in range(NKV):
                            for lh in range(2):
                                i0 = src[HD * g:HD * (g + 1), CMP_D * lh:CMP_D * (lh + NC)].rearrange("p (c l) -> p l c", l=CMP_D)
                                i1 = pe_cols[HD * g:HD * (g + 1), kv, lh * CMP_D:(lh + 1) * CMP_D].rearrange(
                                    "p (l o) -> p l o", o=1).to_broadcast([HD, CMP_D, NC])
                                ins = dve.tensor_tensor(blk[HD * lh:HD * (lh + 1), :, g * NC:(g + 1) * NC], i0, i1, ALU.add)
                        ins.then_inc(blk_made, 1)

                    def silu(kv):
                        dve.wait_ge(hid_sig, kv + 1)
                        dve.tensor_tensor(hsil[:, :, :], hsig[:, :, :], pv[:, :, 0:2 * NC], ALU.mult).then_inc(hid_silu, 1)

                    dve.wait_ge(tab_in, 32)
                    for i in range(2):
                        dve.wait_ge(gate_out[i], 8 * KC)
                    rope("kc")
                    dve.wait_ge(rope_made, 1)
                    blocks(0)
                    rope("q0")
                    silu(0)
                    freed(dve, "vc")
                    blocks(1)
                    rope("q1")
                    silu(1)
                    rope("q2")
                    dve.wait_ge(cmp_made, 3)
                    dve.tensor_tensor(vcmp[:, :, HD:P], pv[0:NC, 0, 256:256 + 2 * HD].rearrange("p (g c) -> p g c", g=NKV),
                                      vcmp[:, :, 0:HD].bitcast(F32), ALU.subtract).then_inc(vc_lo, 1)
                    rope("q3")
                    rope("ks")
                    v_low("vs", vs)
                    rope("kw")
                    dve.wait_ge(aux_done, AUXED.index("nsaT") + 1)
                    dve.tensor_copy(gates[:, :, :].rearrange("p t n -> p (t n)"), aux[:, 0:NT * NG]).then_inc(aux_free, 1)
                    v_low("vw", vw)

                    dve.wait_ge(aux_free, len(AUXED))
                    dve.wait_ge(rope_made, len(ROPED))

                    def bc(t, n):
                        return t.rearrange("p (h o) -> p h o", o=1).to_broadcast([P, t.shape[1], n])

                    then(dve.memset(selb[:, :, :], 0.0))
                    mx8, sum8, r8 = (cst[:, i, :] for i in range(3))
                    c3 = cprob[:, :, 0:NC]

                    def cmp_scores(u, qt):
                        m = cmask[:, 56 - 8 * qt:56 - 8 * qt + NC].rearrange("p (o c) -> p o c", o=1).to_broadcast([P, HPG, NC])
                        if qt:
                            dve.wait_ge(c_exp, qt)
                        for g in range(NKV):
                            s3 = lin[u % 2][:, g * 512:(g + 1) * 512].rearrange("p (h c) -> p h c", h=HPG)[:, :, g * NC:(g + 1) * NC]
                            ins = dve.tensor_tensor(scm[:, HPG * g:HPG * (g + 1), 0:NC], s3, m, ALU.add)
                        then(ins)
                        then(dve.tensor_reduce(mx8, scm[:, :, 0:NC], AX.X, ALU.max))
                        dve.tensor_tensor(scm[:, :, 0:NC], scm[:, :, 0:NC], bc(mx8, NC), ALU.subtract).then_inc(c_in_made, 1)

                    def cmp_probs(qt):
                        dve.wait_ge(c_exp, qt + 1)
                        then(dve.tensor_reduce(sum8, c3, AX.X, ALU.add))
                        then(dve.reciprocal(r8, sum8))
                        if qt == 0:
                            then(dve.tensor_scalar(r8, r8, rowok[:, 0:1], None, ALU.mult))
                        dve.tensor_tensor(c3, c3, bc(r8, NC), ALU.mult).then_inc(c_prob, 1)
                        dve.wait_ge(c_prob, qt + 1)
                        if qt:
                            dve.wait_ge(t_done, C_GROUP[qt - 1, NKV - 1]["no"] + 1)
                        dve.tensor_tensor(cgated[:, :, 0:NC], c3, bc(gates[:, qt, 0:NH], NC), ALU.mult).then_inc(c_gated, 1)
                        if qt == 0:
                            then(dve.memset(psum4[:, :, :], 0.0))
                        p4 = cprob.rearrange("p (g i) c -> p g c i", g=NKV)[:, :, 0:NC, :]
                        then(dve.tensor_reduce(psum4[:, :, 1:1 + NC], p4, AX.X, ALU.add))

                    def select(qt):
                        q4 = psum4[:, :, 1:65].rearrange("p g (n i) -> p g n i", i=4)
                        then(dve.tensor_reduce(imp[:, :, :], q4, AX.X, ALU.add))
                        before = psum4[:, :, 0:64].rearrange("p g (n i) -> p g n i", i=4)[:, :, :, 0]
                        then(dve.tensor_tensor(imp[:, :, :], imp[:, :, :], before, ALU.add))
                        for tab, op in ((vtab, ALU.mult), (ftab, ALU.add)):
                            tb = tab[:, 14 - 2 * qt:14 - 2 * qt + NS].rearrange("p (o n) -> p o n", o=1).to_broadcast([P, NKV, NS])
                            then(dve.tensor_tensor(imp[:, :, :], imp[:, :, :], tb, op))
                        then(dve.memset(imp[:, :, 0:1], 2 * BONUS))
                        for g in range(NKV):
                            ins = dve.max(top8[:, g, :], imp[:, g, :])
                        then(ins)
                        for g in range(NKV):
                            ins = dve.match_replace(left[:, g, :], top8[:, g, :], imp[:, g, :], TAKEN)
                        then(ins)
                        if qt:
                            dve.wait_ge(t_done, B_GROUP[qt - 1]["no"] + 1)
                        dve.tensor_scalar(selb[:, :, 0:NS], left[:, :, :], TAKEN / 10, NEG, ALU.is_lt, ALU.mult).then_inc(sel_made, 1)

                    def factors(st):
                        no, m = st["no"], SCORES_BEFORE[st["first"]]
                        f = fac[:, no % 2, :]
                        dve.wait_ge(exp_made, m + HPG)
                        if no >= 2:
                            dve.wait_ge(p_scaled, HPG * (no - 1))
                        then(dve.reciprocal(f, sums[:, m:m + HPG]))
                        gt = BRANCH[st["b"]] * NH + HPG * st["g"]
                        dve.tensor_tensor(f, f, gates[:, st["qt"], gt:gt + HPG], ALU.mult).then_inc(f_made, 1)

                    for u in range(len(STEPS)):
                        if u < len(UNITS):
                            dve.wait_ge(s_done, u + 1)
                            if UNITS[u][0] == "c":
                                cmp_scores(u, UNITS[u][1])
                            else:
                                st, m = SETS[UNITS[u][4]], SCORES_BEFORE[u]
                                at = chunks(st)[0][2]
                                dve.tensor_reduce(negm[:, m:m + 1], lin[u % 2][:, at:at + st["n"]], AX.X, ALU.max, negate=True).then_inc(max_made, 1)
                        for x in STEPS[u - 1] if u else []:
                            if x["kind"] != "b":
                                r, t = NC if x["kind"] == "c" else P, x["v_no"] % PT
                                dve.wait_ge(t_hi, x["v_no"] + 1)
                                dve.tensor_tensor(pTL[0:r, t, :], pTF[0:r, t, :], pTH[0:r, t, :].bitcast(F32),
                                                  ALU.subtract).then_inc(t_lo, 1)
                        for st in SETS:
                            if st["last"] + 1 == u:
                                factors(st)
                        if 1 <= u <= len(UNITS) and UNITS[u - 1][0] == "c":
                            cmp_probs(UNITS[u - 1][1])
                        if 2 <= u < len(UNITS) + 2 and UNITS[u - 2][0] == "c":
                            select(UNITS[u - 2][1])
                        for st in SETS:
                            if st["b"] != "s":
                                continue
                            k = NKV * st["qt"] + st["g"]
                            if st["fin"] == u:
                                dve.wait_ge(fin_low, k + 1)
                                if k:
                                    dve.wait_ge(fin_lo, k)
                                for odd in range(2):
                                    pick = lambda t: t.rearrange("p (j o t) -> p j o t", j=2, o=2)[:, :, odd, :]
                                    dve.tensor_tensor(att[HD * odd:HD * (odd + 1), :].rearrange("p (j t) -> p j t", j=2),
                                                      pick(pv[0:HD, st["g"], :]), pick(low_half), ALU.add).then_inc(fin_sum, 1)
                            if st["fin"] + 1 == u:
                                dve.wait_ge(o_hi, k + 1)
                                at_ = (slice(None), slice(2 * st["g"], 2 * st["g"] + 2), slice(st["qt"] * P, (st["qt"] + 1) * P))
                                dve.tensor_tensor(atL[at_], att.rearrange("p (j t) -> p j t", j=2), atH[at_].bitcast(F32),
                                                  ALU.subtract).then_inc(fin_lo, 1)

                    for i in range(KC + 1):
                        if i < KC:
                            t = tmp[:, i % 2, :]
                            done(dve, ("ua", i))
                            dve.wait_ge(fetch_sem[i % 2], 32 * (i // 2 + 1))
                            if i >= 2:
                                dve.wait_ge(mg_lo, i - 1)
                            dve.tensor_tensor(t, slot(("ua", i))[:, :], stG[:, i % 2, :], ALU.mult).then_inc(free_sem(("ua", i)), 1)
                            freed(dve, ("ua", i))
                            dve.tensor_tensor(t, t, stM[:, i % 2, :], ALU.add).then_inc(mg_made, 1)
                        if i:
                            dve.wait_ge(mg_hi, i)
                            dve.tensor_tensor(mxL[:, i - 1, :], tmp[:, (i - 1) % 2, :], mxH[:, i - 1, :].bitcast(F32),
                                              ALU.subtract).then_inc(mg_lo, 1)

                    def add_squares(i, n):
                        if i:
                            dve.wait_ge(sq_made, n * KC + i + 1)
                            dve.tensor_tensor(tmp[:, 0, :], tmp[:, 0, :], tmp[:, 1, :], ALU.add).then_inc(ss_added, 1)
                            dve.wait_ge(ss_added, n * (KC - 1) + i)

                    n_x = [0]

                    def residual(name, gate, i):
                        done(dve, name)
                        dve.scalar_tensor_tensor(out=xT[:, i, :], in0=slot(name)[:, :], scalar=adac[:, gate + i:gate + i + 1],
                                                 in1=xT[:, i, :], op0=ALU.mult, op1=ALU.add).then_inc(x_made, 1)
                        n_x[0] += 1
                        dve.wait_ge(x_made, n_x[0])
                        dve.sem_inc(free_sem(name), 1)

                    dve.wait_ge(x_back, 16)
                    for i in range(KC + 1):
                        if i < KC:
                            residual(("wo", i), 2 * KC, i)
                        if i:
                            add_squares(i - 1, 0)
                    norm(1)

                    def ff1(fg):
                        for f in range(FG * fg, FG * fg + FG):
                            if f < ADA_FIRST:
                                ada()
                            dve.wait_ge(relu_made, f + 1)
                            if f:
                                dve.wait_ge(hid_lo, f)
                            dve.tensor_tensor(tmp[:, 1, :], tmp[:, 0, :], tmp[:, 0, :], ALU.mult).then_inc(hid_sq, 1)
                            dve.wait_ge(hid_sq, f + 1)
                            dve.wait_ge(hid_hi, f + 1)
                            dve.tensor_tensor(hidL[:, fg % 2, f % FG, :], tmp[:, 1, :], hidH[:, fg % 2, f % FG, :].bitcast(F32),
                                              ALU.subtract).then_inc(hid_lo, 1)

                    ff1(0)
                    for fg in range(NFG):
                        if fg + 1 < NFG:
                            ff1(fg + 1)
                        for i in range(KC):
                            residual(("f2", fg, i), 5 * KC, i)
                            if fg == NFG - 1 and i:
                                add_squares(i - 1, 1)
                    add_squares(KC - 1, 1)
                    dve.wait_ge(ada_mm, NADA)
                    dve.tensor_copy(adac[:, 0:ADA_FIRST], pv[:, 0, 0:ADA_FIRST]).then_inc(par_c, 1)

            clear()

        f_t, f_tr, f_ev, f_out = sem("f_t"), sem("f_tr"), sem("f_ev"), sem("f_out")
        with nc.Block() as block:
            @block.tensor
            def _(pe):
                for hf in half:
                    mm = pe.matmul(aux[:, hf], ones[:, :], tmp[:, 0, hf], start=True, stop=True)
                mm.then_inc(ss_done, 1)
                for g in range(2 * NT):
                    t, hh = g // 2, g % 2
                    pe.wait_ge(f_t, KC)
                    if g >= 4:
                        pe.wait_ge(f_ev, g - 3)
                    for i in range(4):
                        at = hh * 512 + i * P
                        mm = pe.transpose(lin[t % 2][:, at:at + P], xT[:, 4 * hh + i, t * P:(t + 1) * P], ident[:, :])
                    mm.then_inc(f_tr, 1)

            @block.scalar
            def _(act):
                act.wait_ge(mean_made, 1)
                act.activation(tmp[:, 1, :], tmp[:, 0, :], ACT.Sqrt).then_inc(root_made, 1)

            @block.vector
            def _(dve):
                dve.wait_ge(ss_done, 1)
                dve.tensor_scalar(tmp[:, 0, :], aux[:, :], 1.0 / D, EPS, ALU.mult, ALU.add).then_inc(mean_made, 1)
                dve.wait_ge(root_made, 1)
                dve.reciprocal(tmp[:, 0, :], tmp[:, 1, :]).then_inc(rstd_made, 1)
                dve.wait_ge(rstd_made, 1)
                for k in range(KC):
                    dve.scalar_tensor_tensor(out=xT[:, k, :], in0=xT[:, k, :], scalar=cols[:, R_GFIN + k:R_GFIN + k + 1],
                                             in1=tmp[:, 0, :], op0=ALU.mult, op1=ALU.mult).then_inc(f_t, 1)
                for g in range(2 * NT):
                    t, hh = g // 2, g % 2
                    dve.wait_ge(f_tr, g + 1)
                    dve.tensor_copy(outb[:, t, half[hh]], lin[t % 2][:, half[hh]]).then_inc(f_ev, 1)

            @block.sync
            def _(sp):
                for t in range(NT):
                    sp.wait_ge(f_ev, 2 * t + 2)
                    sp.dma_start(out[0, t * P:(t + 1) * P, :], outb[:, t, :]).then_inc(f_out, 16)
                sp.wait_ge(f_out, 16 * NT)


_INS = ["x", "c", "positions", "w_ada", "b_ada", "g_mix", "w_in", "b_in", "conv_w", "cmp_k_w1", "cmp_k_w2", "cmp_k_pe",
        "cmp_v_w1", "cmp_v_w2", "cmp_v_pe", "w_up_conv", "w_up_attn", "w_o", "g_mlp", "w_ff1", "w_ff2", "g_final"]


def kernel(**inputs):
    import concourse.bacc as _bacc
    from concourse.bass_utils import run_bass_kernel_spmd as _run

    nc = _bacc.Bacc("TRN2", target_bir_lowering=False, num_devices=1)
    arrays, aps = {}, {}
    for name in _INS:
        arr = np.ascontiguousarray(inputs[name])
        arrays[f"in_{name}"] = arr
        aps[name] = nc.dram_tensor(f"in_{name}", arr.shape, mybir.dt.from_np(arr.dtype), kind="ExternalInput").ap()
    out = nc.dram_tensor("out_x", (1, SEQ, D), F32, kind="ExternalOutput").ap()
    trunk(nc, aps, out)
    r = _run(nc, [arrays], core_ids=[0])
    return r.results[0]["out_x"]
```

```python
from contextlib import ExitStack

import numpy as np

import concourse.bass as bass
from concourse import mybir

F32 = mybir.dt.float32
F32R = mybir.dt.float32r
BF16 = mybir.dt.bfloat16
I32 = mybir.dt.int32
ALU = mybir.AluOpType
ACT = mybir.ActivationFunctionType
AX = mybir.AxisListType

P = 128
DEPTH, SEQ, D = 2, 1024, 1024
KC = D // P
NT = SEQ // P
CONV_W, CONV_K = 512, 3
NH, HD, NKV = 8, 64, 2
HPG = NH // NKV
CMP_L, CMP_D, CMP_H = 32, 16, 256
NC = (SEQ - CMP_L) // CMP_D + 1
SEL_L, N_SEL = 64, 8
NS = SEQ // SEL_L
WIN_T = 512 // P
D_FF = 4 * D
FG = 4
NFG = D_FF // (FG * P)
NADA = 6 * KC
EPS = 1e-6
NEG = -1e30
BONUS = 1e4
TAKEN = 1e30
SCALE = HD ** -0.5
THETA = 10000.0

O_CB, O_CC, O_CU = 0, CONV_W, 2 * CONV_W
O_Q = 3 * CONV_W
O_KC, O_VC, O_KS, O_VS, O_KW, O_VW = (O_Q + NH * HD + i * NKV * HD for i in range(6))
O_NSA = O_VW + NKV * HD
NG = 3 * NH
O_MG = O_NSA + NG
IN_W = O_MG + 2 * D

R_ADA = 0
R_BIN = R_ADA + NADA
R_NSA = R_BIN + O_NSA // P
R_MG = R_NSA + 1
R_GMIX = R_MG + 2 * KC
R_GMLP = R_GMIX + KC
R_CONV = R_GMLP + KC
R_GFIN = R_CONV + CONV_K * CONV_W // P
R_END = R_GFIN + KC

RAW = 3
SPL = 2
ADA_FIRST = 2 * KC
CMP_T = 4
LPT = CMP_L // 2 // CMP_T


def weight_plan():
    tiles, chunk = [], {}
    ada = iter(range(ADA_FIRST, NADA))

    def dense(src, row, col, names, with_ada=False):
        for n in names:
            chunk[n] = len(chunk)
        tiles.append(("split", src, row, col, 8 // len(names), names))
        if with_ada:
            tiles.append(("ada", next(ada)))

    for j in range(CONV_W // P):
        for name, off in (("cc", O_CC), ("cu", O_CU), ("cb", O_CB)):
            dense("w_in", 0, off + P * j, [(name, j)], True)
    for i in range(0, KC, 2):
        dense("w_in", 0, O_MG + P * i, [("gc", i)], True)
        dense("w_in", 0, O_MG + P * (i + 1), [("gc", i + 1)], True)
        dense("w_up_conv", 0, P * i, [("uc", i), ("uc", i + 1)], True)
    for i in range(KC):
        dense("w_in", 0, O_MG + D + P * i, [("ga", i)], True)
    assert next(ada, None) is None
    for name, off in (("kc", O_KC), ("vc", O_VC), ("q0", O_Q), ("q1", O_Q + P), ("q2", O_Q + 2 * P)):
        dense("w_in", 0, off, [name])
    tiles += [("cmp", 0, t) for t in range(CMP_T)]
    dense("w_in", 0, O_Q + 3 * P, ["q3"])
    tiles += [("cmp", 1, t) for t in range(CMP_T)]
    for name, off in (("ks", O_KS), ("vs", O_VS), ("kw", O_KW), ("ns", O_NSA), ("vw", O_VW)):
        dense("w_in", 0, off, [name])
    for i in range(0, KC, 2):
        dense("w_up_attn", 0, P * i, [("ua", i), ("ua", i + 1)])
    for i in range(KC):
        dense("w_o", 0, P * i, [("wo", i)])

    def ff1(fg):
        for f in range(FG * fg, FG * fg + FG):
            dense("w_ff1", 0, P * f, [("f1", f)])
            if f < ADA_FIRST:
                tiles.append(("ada", f))

    ff1(0)
    for fg in range(NFG):
        if fg + 1 < NFG:
            ff1(fg + 1)
        for i in range(0, KC, 2):
            dense("w_ff2", FG * P * fg, P * i, [("f2", fg, i), ("f2", fg, i + 1)])
    return tiles, chunk


TILES, CHUNK = weight_plan()
IN_SLOT, SPLIT_NO, KIND_NO = [], {}, []
_count = [0] * RAW
for _n, _t in enumerate(TILES):
    _count[_n % RAW] += 32 if _t[0] == "cmp" else 16
    IN_SLOT.append(_count[_n % RAW])
    KIND_NO.append(sum(t[0] == _t[0] for t in TILES[:_n]))
    if _t[0] == "split":
        SPLIT_NO[_n] = KIND_NO[_n]
TILE_OF = {}
for _n, _t in enumerate(TILES):
    if _t[0] == "split":
        for _name in _t[5]:
            TILE_OF[_name] = _n
    else:
        TILE_OF[_t] = _n


def attention_plan():
    units, sets, flush = [("c", NT - 1)], [], []
    for qt in reversed(range(NT)):
        for g in range(NKV):
            for b in ("w", "s"):
                if b == "s" and g == NKV - 1 and qt:
                    units.append(("c", qt - 1))
                lo = max(0, qt - WIN_T) if b == "w" else 0
                sets.append(dict(no=len(sets), b=b, qt=qt, g=g, lo=lo, n=(qt + 1 - lo) * P, first=len(units)))
                units += [(b, qt, g, i, len(sets) - 1) for i in range(HPG)]
                sets[-1]["last"] = len(units) - 1
    steps = [[] for _ in range(len(units) + T_AFTER + 3)]
    for s in sets:
        keys = list(range(s["lo"], s["qt"] + 1))
        e = s["last"]
        if s["b"] == "w" and s["g"] == 0 and s["qt"] >= CHOICE:
            steps[e - 1].append(dict(kind="b", qt=s["qt"]))
        per = max(2, -(-len(keys) // 4))
        if s["b"] == "w":
            steps[e].append(dict(kind="c", qt=s["qt"], g=s["g"], first=True, last=False))
        for i, key in enumerate(keys):
            steps[e + T_AFTER + i // per].append(dict(kind="p", set=s, qt=s["qt"], g=s["g"], key=key, at=i * P, first=False,
                                                last=s["b"] == "s" and key == s["qt"], end=key == s["qt"]))
    groups = []
    for here in steps:
        for g in here:
            g.update(no=len(groups), bank=len(groups) % 2, v_no=sum(x["kind"] != "b" for x in groups))
            groups.append(g)
    waiting = []
    for u, here in enumerate(steps):
        for g in here:
            waiting += [g] * (g["kind"] != "b")
            g["then"] = [waiting.pop(0) for _ in range(len(waiting) - V_AFTER)]
        rest = []
        if not here or u == len(steps) - 1:
            rest, waiting = waiting, []
        flush.append(rest)
        for g in [v for x in here for v in x["then"]] + rest:
            if g["kind"] == "p" and g["last"]:
                g["set"]["fin"] = u + 1
    steps += [[], [], [], []]
    flush += [[], [], [], []]
    return units, sets, steps, flush, groups


CHOICE = N_SEL * SEL_L // P
V_AFTER = 3
SCALED_AFTER = (1, 2, 3, 3)
T_AFTER = 5

def score_banks(units):
    banks, last, step = [], [], []
    for u, x in enumerate(units):
        narrow = x[0] != "c" and x[1] < CHOICE
        banks.append([u % 4] if narrow else [u % 2 * 2, u % 2 * 2 + 1])
        last.append([v for v in range(u) if set(banks[v]) & set(banks[u])][-1:])
        step.append(max([u - 2, 0] + [v + 1 for v in last[u]] + step[-1:]))
    return banks, last, step


UNITS, SETS, STEPS, FLUSH, GROUPS = attention_plan()
BANKS, BANK_LAST, SCORE_STEP = score_banks(UNITS)
SCORES_BEFORE = [sum(x[0] != "c" for x in UNITS[:u]) for u in range(len(UNITS) + 1)]
END_GROUP = {g["set"]["no"]: g for g in GROUPS if g["kind"] == "p" and g["end"]}
C_GROUP = {(g["qt"], g["g"]): g for g in GROUPS if g["kind"] == "c"}
B_GROUP = {g["qt"]: g for g in GROUPS if g["kind"] == "b"}
N_VGROUPS = sum(g["kind"] != "b" for g in GROUPS)
PROBS = 3
PT = 4
NTH = {qt: NT - 1 - qt for qt in range(NT)}
SEEN = {qt: (qt + 1) * P // CMP_D - 1 for qt in range(NT)}
BRANCH = {"c": 0, "s": 1, "w": 2}


def trunk(nc, a, out):
    with ExitStack() as ctx:
        def sb(name, shape, dt=F32):
            return ctx.enter_context(nc.sbuf_tensor(name, shape, dt))

        def region(name, words, *layouts):
            found = []
            for layout in layouts:
                with ExitStack() as s:
                    found.append([s.enter_context(nc.sbuf_tensor(n, sh, dt)) for n, sh, dt in layout])
            sb(name, [P, words])
            return found

        every = []

        def sem(name):
            every.append(ctx.enter_context(nc.semaphore(name)))
            return every[-1]

        other = TILE_OF[("ua", 4)] % RAW
        before = [("before", [P, other * 1024], F32)] * (other > 0)
        (wraw,), pt_r, pt_f = region("r_raw", RAW * 1024, [("wraw", [P, RAW, 1024], F32)],
                                     before + [("pTH3", [P, 512], F32R), ("pTL3", [P, 512], F32R)],
                                     [(n + "_", sh, dt) for n, sh, dt in before] + [("pTH3_", [P, 512], F32R), ("pTF3", [P, 512], F32)])
        (whi, wlo), (prob3,) = region("r_w", 2 * SPL * 1024, [(n, [P, SPL, 1024], F32R) for n in ("whi", "wlo")],
                                      [("prob3", [P, HPG, SEQ], F32)])
        tmp = sb("tmp", [P, 2, SEQ])
        (xT,), (cosT, sinT, kcT, vcT, fbuf, ropes), (vw, vs, pTH, pTL, scm, psum4, negm, sums, cst, imp, top8, left, fac), (_, _, _, pTF) = region(
            "r_x", KC * SEQ, [("xT", [P, KC, SEQ], F32)],
            [("cosT", [P, SEQ], F32), ("sinT", [P, SEQ], F32), ("kcT", [P, SEQ], F32), ("vcT", [P, SEQ], F32),
             ("fbuf", [P, 2, SEQ], F32), ("ropes", [P, 2, SEQ], F32)],
            [("vw", [P, NT, NKV, P], F32R), ("vs", [P, NT, NKV, P], F32R), ("pTH", [P, PT - 1, 512], F32R),
             ("pTL", [P, PT - 1, 512], F32R), ("scm", [P, NH, 64], F32), ("psum4", [P, NKV, 65], F32),
             ("negm", [P, len(UNITS) - NT], F32), ("sums", [P, len(UNITS) - NT], F32), ("cst", [P, 3, NH], F32),
             ("imp", [P, NKV, NS], F32), ("top8", [P, NKV, 8], F32), ("left", [P, NKV, NS], F32),
             ("fac", [P, 2, HPG], F32)],
            [("vw_", [P, NT, NKV, P], F32R), ("vs_", [P, NT, NKV, P], F32R), ("pTH_", [P, PT - 1, 512], F32R),
             ("pTF", [P, PT - 1, 512], F32)])
        (hH, hL), (atH, atL, prob), (_, _, stG, stM), (xin,) = region(
            "r_h", 2 * KC * SEQ, [("hH", [P, KC, SEQ], F32R), ("hL", [P, KC, SEQ], F32R)],
            [("atH", [P, 4, SEQ], F32R), ("atL", [P, 4, SEQ], F32R), ("prob", [P, 2, HPG, SEQ], F32)],
            [("atH_", [P, 4, SEQ], F32R), ("atL_", [P, 4, SEQ], F32R), ("stG", [P, 2, SEQ], F32),
             ("stM", [P, 2, SEQ], F32)],
            [("xin", [P, NT, D], F32)])
        (qS, kwH, kwL, ksH, ksL), (_, blk, w2, pe_rows), (cvH, cvL), (mxH, mxL), (hidH, hidL), (nt, nf, crow), (outb,) = region(
            "r_m", 2 * KC * SEQ,
            [("qS", [P, NH, SEQ], F32R)] + [(n, [P, NKV, SEQ], F32R) for n in ("kwH", "kwL", "ksH", "ksL")],
            [("qS_", [P, NH, SEQ], F32R), ("blk", [P, CMP_L // 2, NKV * 64], F32), ("w2", [P, 2, 2, HD], F32),
             ("pe_rows", [CMP_L, 2 * P], F32)],
            [("cvH", [P, 4, SEQ], F32R), ("cvL", [P, 4, SEQ], F32R)],
            [("mxH", [P, KC, SEQ], F32R), ("mxL", [P, KC, SEQ], F32R)],
            [("hidH", [P, 2, FG, SEQ], F32R), ("hidL", [P, 2, FG, SEQ], F32R)],
            [("nt", [P, 2, SEQ], F32), ("nf", [P, 2, SEQ], F32), ("crow", [KC, P], F32)],
            [("outb", [P, NT, D], F32)])

        ident = sb("ident", [P, P])
        identb = sb("identb", [P, P], BF16)
        ones = sb("ones", [P, P])
        rot = sb("rot", [P, P])
        causal = sb("causal", [P, P], BF16)
        oldest = sb("oldest", [P, P], BF16)
        cmask = sb("cmask", [P, 120])
        vtab = sb("vtab", [P, 30])
        ftab = sb("ftab", [P, 30])
        rowok = sb("rowok", [P, 1])
        vecs = sb("vecs", [P, P])
        cols = sb("cols", [P, P])
        pe_cols = sb("pe_cols", [P, 2, CMP_L])
        adac = sb("adac", [P, NADA])
        modA = sb("modA", [P, 2, KC])
        qbias = sb("qbias", [P, 4])
        rms = sb("rms", [P, NT])
        cT = sb("cT", [P, KC])
        csig = sb("csig", [P, KC])
        hsig, hsil = (tmp[:, 0, i * 256:i * 256 + 4 * NC].rearrange("p (i c) -> p i c", i=2) for i in range(2))
        low_half = tmp[0:HD, 0, 0:512]
        att = tmp[:, 0, 512:768]
        gates = tmp[:, 0, 768:768 + NT * NG].rearrange("p (t n) -> p t n", t=NT)
        selb = tmp[:, 0, 768 + NT * NG:SEQ].rearrange("p (g n) -> p g n", g=NKV)
        cprob, cgated = (tmp[:, 1, i * 512:(i + 1) * 512].rearrange("p (h c) -> p h c", h=NH) for i in range(2))
        kcmp = sb("kcmp", [P, NKV * NC])
        vcmp = sb("vcmp", [NC, NKV, P], F32R)
        blocks_of = sb("blocks_of", [P, SEQ], BF16)
        selT = sb("selT", [P, 2, NKV, P], BF16)
        adared = sb("adared", [P, 2, P])

        lin = [ctx.enter_context(nc.psum_tensor(f"lin{i}", [P, SEQ], F32)) for i in range(2)]
        aux = ctx.enter_context(nc.psum_tensor("aux", [P, SEQ], F32))
        pv = ctx.enter_context(nc.psum_tensor("pv", [P, 2, 512], F32))

        def scores(u):
            return lin[BANKS[u][0] // 2][:, BANKS[u][0] % 2 * 512:SEQ]

        def prob_of(no, i):
            if no % PROBS < 2:
                return prob[:, no % PROBS, i, :]
            return prob3[:, i, :]

        def pt(kind, x, r=P):
            t = x["v_no"] % PT
            if t == PT - 1:
                return dict(high=pt_r[-2], low=pt_r[-1], both=pt_f[-1])[kind][0:r, :]
            return dict(high=pTH, low=pTL, both=pTF)[kind][0:r, t, :]

        x_keep = nc.dram_tensor("x_keep", [P, KC, SEQ], F32).ap()
        rope_keep = nc.dram_tensor("rope_keep", [2, P, SEQ], F32).ap()
        mix_keep = nc.dram_tensor("mix_keep", [KC, P, SEQ], F32).ap()
        gate_keep = nc.dram_tensor("gate_keep", [KC, P, SEQ], F32).ap()

        half = [slice(0, 512), slice(512, SEQ)]

        x_in, c_in, pos_in = sem("x_in"), sem("c_in"), sem("pos_in")
        tab_made, pool_step = sem("tab_made"), sem("pool_step")
        p_tr, p_ev = sem("p_tr"), sem("p_ev")
        p_small, p_vec, p_act = sem("p_small"), sem("p_vec"), sem("p_act")
        sq_made, ss_added, ss_done = sem("sq_made"), sem("ss_added"), sem("ss_done")
        rope_out, dve_p = sem("rope_out"), sem("dve_p")
        par_in = sem("par_in")
        raw_in = [sem(f"raw_in{i}") for i in range(RAW)]
        ada_prod, ada_used, ada_mm = sem("ada_prod"), sem("ada_used"), sem("ada_mm")
        posr = tmp[0:1, 0, :]
        invr = cols[0:1, :]

        N_ROWS = 8

        def load_vectors(eng, layer):
            def rows(r, n, src):
                eng.dma_start(vecs[r:r + n, 0:src.shape[-1]], src).then_inc(par_in, 16)

            rows(R_ADA, NADA, a["b_ada"][layer, :].rearrange("(r p) -> r p", p=P))
            rows(R_BIN, O_NSA // P, a["b_in"][layer, 0:O_NSA].rearrange("(r p) -> r p", p=P))
            rows(R_NSA, 1, a["b_in"][layer, O_NSA:O_MG].rearrange("(r p) -> r p", p=NG))
            rows(R_MG, 2 * KC, a["b_in"][layer, O_MG:IN_W].rearrange("(r p) -> r p", p=P))
            rows(R_GMIX, KC, a["g_mix"][layer, :].rearrange("(r p) -> r p", p=P))
            rows(R_GMLP, KC, a["g_mlp"][layer, :].rearrange("(r p) -> r p", p=P))
            rows(R_CONV, CONV_K * CONV_W // P, a["conv_w"][layer, :, :].rearrange("k (j p) -> (k j) p", p=P))
            rows(R_GFIN, KC, a["g_final"].rearrange("(r p) -> r p", p=P))

        def ada_tile(layer, j):
            return a["w_ada"][layer, :, P * j:P * (j + 1)].rearrange("(k p) n -> p k n", p=P)

        def ada_products(dve, n, no, arrived):
            w = wraw[:, n % RAW, :].rearrange("p (k n) -> p k n", k=KC)
            dve.wait_ge(raw_in[n % RAW], arrived)
            dve.tensor_tensor(w, w, cT[:, :].rearrange("p (k o) -> p k o", o=1).to_broadcast([P, KC, P]),
                              ALU.mult).then_inc(ada_prod, 1)
            dve.wait_ge(ada_prod, no + 1)
            if no >= 2:
                dve.wait_ge(ada_mm, no - 1)
            dve.tensor_reduce(adared[:, no % 2, :], w.rearrange("p k n -> p n k"), AX.X, ALU.add).then_inc(ada_used, 1)

        def ada_column(pe, out_col, no):
            pe.wait_ge(ada_used, no + 1)
            pe.matmul(out_col, adared[:, no % 2, :], ones[:, 0:1], start=True, stop=True).then_inc(ada_mm, 1)

        def sum_squares(pe, first, last):
            for i, wait in enumerate((first, last)):
                wait()
                for t in range(NT):
                    mm = pe.matmul(aux[:, t:t + 1], tmp[:, i, t * P:(t + 1) * P], ones[:, 0:1],
                                   start=i == 0 and t == 0, stop=i == 1 and t == NT - 1, skip_group_check=True)
            mm.then_inc(ss_done, 1)

        with nc.Block() as block:
            @block.sync
            def _(sp):
                sp.dma_start(crow[:, :], a["c"][0, :].rearrange("(k p) -> k p", p=P)).then_inc(c_in, 16)
                sp.dma_start(posr.bitcast(I32), a["positions"]).then_inc(pos_in, 16)
                for t in range(NT):
                    sp.dma_start(xin[:, t, :], a["x"][0, t * P:(t + 1) * P, :]).then_inc(x_in, 16)
                for j in range(ADA_FIRST):
                    if j >= RAW:
                        sp.wait_ge(ada_used, j - RAW + 1)
                    sp.dma_start(wraw[:, j % RAW, :].rearrange("p (k n) -> p k n", k=KC), ada_tile(0, j)).then_inc(raw_in[j % RAW], 16)
                sp.wait_ge(p_vec, 3)
                sp.dma_start(rope_keep[0], nt[:, 0, :]).then_inc(rope_out, 16)
                sp.wait_ge(p_act, 4)
                sp.dma_start(rope_keep[1], nt[:, 1, :]).then_inc(rope_out, 16)
                sp.wait_ge(rope_out, 32)

            @block.gpsimd
            def _(pool):
                n = [0]

                def then(ins):
                    n[0] += 1
                    ins.then_inc(pool_step, 1)
                    pool.wait_ge(pool_step, n[0])

                def keep(t, cond, pattern, base, cm, fill):
                    then(pool.affine_select(out=t, in_=t, pattern=pattern, compare_op=cond, fill=fill,
                                            base=base, channel_multiplier=cm))

                for t in (ident, identb):
                    then(pool.memset(t[:, :], 0.0))
                    keep(t[:, :], ALU.not_equal, [[-1, P]], 0, 1, 1.0)
                then(pool.memset(ones[:, :], 1.0))
                then(pool.memset(vecs[:, :], 0.0))
                for i in range(HD // 2):
                    f = float(np.float32(THETA) ** np.float32(-i * 2.0 / HD))
                    ins = pool.memset(invr.rearrange("o (r i) -> o r i", r=4)[:, :, i:i + 1], f)
                    then(ins)
                pool.sem_inc(tab_made, 1)
                then(pool.memset(rot[:, :], 0.0))
                rv = rot[:, :].rearrange("p (a i) -> p a i", a=2)
                keep(rv[:, :, 0:32], ALU.not_equal, [[-64, 2], [-1, 32]], -32, 1, -1.0)
                keep(rv[:, :, 32:64], ALU.not_equal, [[-64, 2], [-1, 32]], 0, 1, 1.0)
                then(pool.memset(causal[:, :], 0.0))
                keep(causal[:, :], ALU.is_ge, [[-1, P]], 0, 1, NEG)
                then(pool.memset(oldest[:, :], 0.0))
                keep(oldest[:, :], ALU.is_ge, [[1, P]], -1, -1, NEG)
                then(pool.memset(cmask[:, :], 0.0))
                keep(cmask[:, :], ALU.is_ge, [[-CMP_D, 120]], CMP_D * 56 - CMP_L + 1, 1, NEG)
                then(pool.memset(vtab[:, :], 1.0))
                keep(vtab[:, :], ALU.is_ge, [[-SEL_L, 30]], SEL_L * 14, 1, 0.0)
                then(pool.memset(ftab[:, :], BONUS))
                keep(ftab[:, :], ALU.is_ge, [[SEL_L, 30]], P - 1 - SEL_L * 14, -1, 0.0)
                keep(ftab[:, :], ALU.is_ge, [[-SEL_L, 30]], SEL_L * 14, 1, -1.0)
                then(pool.memset(rowok[:, :], 1.0))
                keep(rowok[:, :], ALU.is_ge, [[0, 1]], -(CMP_L - 1), 1, 0.0)
                then(pool.memset(selT[:, :, :, :], 0.0))
                then(pool.memset(blocks_of[:, :], 1.0))
                keep(blocks_of[:, :], ALU.is_ge, [[1, SEQ]], 0, -SEL_L, 0.0)
                keep(blocks_of[:, :], ALU.is_ge, [[-1, SEQ]], SEL_L - 1, SEL_L, 0.0)
                for k in range(1, KC - 1):
                    pool.wait_ge(sq_made, k + 1)
                    pool.tensor_tensor(tmp[:, 0, :], tmp[:, 0, :], tmp[:, 1, :], ALU.add).then_inc(ss_added, 1)
                    pool.wait_ge(ss_added, k)

            @block.tensor
            def _(pe):
                pe.wait_ge(tab_made, 1)
                pe.wait_ge(c_in, 16)
                pe.transpose(pv[:, 0, 0:KC], crow[:, :], ident[0:KC, 0:KC])
                pe.matmul(pv[:, 0, 64:65], invr, ones[0:1, 0:1], start=True, stop=True).then_inc(p_small, 1)
                pe.wait_ge(p_vec, 1)
                for hf in half:
                    mm = pe.matmul(aux[:, hf], ones[0:1, :], tmp[0:1, 1, hf], start=True, stop=True)
                mm.then_inc(p_small, 1)
                for g in range(2 * KC):
                    k, hh = g // 2, g % 2
                    if g >= 4:
                        pe.wait_ge(p_ev, g - 3)
                    pe.wait_ge(x_in, 16 * NT)
                    for t in range(4):
                        tt = 4 * hh + t
                        mm = pe.transpose(lin[g // 2 % 2][:, g % 2 * 512 + t * P:g % 2 * 512 + (t + 1) * P],
                                          xin[:, tt, k * P:(k + 1) * P], ident[:, :])
                    mm.then_inc(p_tr, 1)
                    if g % 2 and k:
                        ada_column(pe, pv[:, 1, k - 1:k], k - 1)
                for j in range(KC - 1, ADA_FIRST):
                    if j == ADA_FIRST - 6:
                        sum_squares(pe, lambda: pe.wait_ge(ss_added, KC - 2), lambda: pe.wait_ge(sq_made, KC))
                    ada_column(pe, pv[:, 1, j:j + 1], j)

            @block.scalar
            def _(act):
                act.wait_ge(tab_made, 1)
                load_vectors(act, 0)
                act.wait_ge(p_small, 1)
                act.activation(csig[:, :], pv[:, 0, 0:KC], ACT.Sigmoid).then_inc(p_act, 1)
                act.wait_ge(p_vec, 2)
                act.activation(nt[:, 1, :], nf[:, 0, :], ACT.Sin).then_inc(p_act, 1)
                act.activation(nf[:, 1, :], nf[:, 0, :], ACT.Sin, scale=0.5).then_inc(p_act, 1)
                act.wait_ge(p_act, 3)
                act.activation(nf[:, 0, :], nf[:, 1, :], ACT.Square).then_inc(p_act, 1)
                act.wait_ge(p_vec, 3)
                for g in range(2 * KC):
                    k, hh = g // 2, g % 2
                    act.wait_ge(p_tr, g + 1)
                    act.activation(xT[:, k, half[hh]], lin[k % 2][:, half[hh]], ACT.Copy).then_inc(p_ev, 1)
                    if g % 2:
                        act.wait_ge(p_ev, g + 1)
                        if k >= 2:
                            act.wait_ge(ss_added, k - 1)
                        act.activation(tmp[:, min(k, 1), :], xT[:, k, :], ACT.Square).then_inc(sq_made, 1)
                act.wait_ge(par_in, 16 * N_ROWS)

            @block.vector
            def _(dve):
                n = [0]

                def then(ins):
                    n[0] += 1
                    ins.then_inc(dve_p, 1)
                    dve.wait_ge(dve_p, n[0])

                dve.wait_ge(pos_in, 16)
                dve.tensor_copy(tmp[0:1, 1, :], posr.bitcast(I32)).then_inc(p_vec, 1)
                dve.wait_ge(p_act, 1)
                dve.tensor_tensor(cT[:, :], csig[:, :], pv[:, 0, 0:KC], ALU.mult).then_inc(dve_p, 1)
                n[0] += 1
                inv = qbias[:, 0:1]
                then(dve.tensor_copy(inv, pv[:, 0, 64:65]))
                dve.wait_ge(p_small, 2)
                ang, turns = nf[:, 0, :], nf[:, 1, :]
                then(dve.tensor_scalar(ang, aux[:, :], inv, None, ALU.mult))
                magic = 1.5 * 2.0 ** 23
                then(dve.tensor_scalar(turns, ang, 1.0 / (2 * np.pi), magic, ALU.mult, ALU.add))
                then(dve.tensor_scalar(turns, turns, magic, None, ALU.subtract))
                rest = 2 * np.pi
                for bits in (8, 8, 8, 24):
                    e = int(np.floor(np.log2(rest)))
                    part = float(np.float32(np.floor(rest / 2.0 ** (e - bits + 1)) * 2.0 ** (e - bits + 1)))
                    rest -= part
                    then(dve.scalar_tensor_tensor(out=ang, in0=turns, scalar=-part, in1=ang,
                                                  op0=ALU.mult, op1=ALU.add))
                pi = float(np.nextafter(np.float32(np.pi), np.float32(0)))
                dve.tensor_scalar(ang, ang, -pi, pi, ALU.max, ALU.min).then_inc(p_vec, 1)
                dve.wait_ge(p_act, 4)
                dve.tensor_scalar(nt[:, 0, :], nf[:, 0, :], -2.0, 1.0, ALU.mult, ALU.add).then_inc(p_vec, 1)
                for j in range(ADA_FIRST):
                    ada_products(dve, j, j, 16 * (j // RAW + 1))
                dve.wait_ge(ada_mm, ADA_FIRST)
                dve.tensor_copy(adac[:, 0:ADA_FIRST], pv[:, 1, 0:ADA_FIRST]).then_inc(p_vec, 1)

        cmp_in, x_out, tab_in, dve_step = (sem(s) for s in ("cmp_in", "x_out", "tab_in", "dve_step"))
        mix_out, gate_out = ([sem(f"{n}{i}") for i in range(2)] for n in ("mix_out", "gate_out"))
        fetch_sem = [sem(f"fetch{i}") for i in range(2)]
        x_back = sem("x_back")
        w_hi, w_split, cmp_used = sem("w_hi"), sem("w_split"), sem("cmp_used")
        lin_done = sem("lin_done")
        lin_free = [sem(f"lin_free{i}") for i in range(2)]
        par_t, ada_cols = (sem(s) for s in ("par_t", "ada_cols"))
        mean_made, root_made, rstd_made, diag_made, spread = (sem(s) for s in ("mean_made", "root_made", "rstd_made", "diag_made", "spread"))
        h_t, h_hi, h_lo = (sem(s) for s in ("h_t", "h_hi", "h_lo"))
        conv_made, cv_hi, cv_lo = (sem(s) for s in ("conv_made", "cv_hi", "cv_lo"))
        z_made, aux_done, aux_free, rope_made, blk_made = (sem(s) for s in ("z_made", "aux_done", "aux_free", "rope_made", "blk_made"))
        hid_sig, hid_silu, cmp_done, cmp_made = (sem(s) for s in ("hid_sig", "hid_silu", "cmp_done", "cmp_made"))
        rope_sum, rope_hi, v_hi, vc_lo = (sem(s) for s in ("rope_sum", "rope_hi", "v_hi", "vc_lo"))
        f_made, p_scaled = sem("f_made"), sem("p_scaled")
        t_hi, t_lo, fin_low, fin_sum, fin_lo = (sem(s) for s in ("t_hi", "t_lo", "fin_low", "fin_sum", "fin_lo"))
        s_done, max_made, exp_made = (sem(s) for s in ("s_done", "max_made", "exp_made"))
        c_in_made, c_exp, sel_made = (sem(s) for s in ("c_in_made", "c_exp", "sel_made"))
        c_gated, t_done, v_done, o_hi = (sem(s) for s in ("c_gated", "t_done", "v_done", "o_hi"))
        t_free = [sem(f"t_free{i}") for i in range(2)]
        mg_made, mg_hi, mg_lo = (sem(s) for s in ("mg_made", "mg_hi", "mg_lo"))
        x_made, relu_made, hid_sq, hid_hi, hid_lo = (sem(s) for s in ("x_made", "relu_made", "hid_sq", "hid_hi", "hid_lo"))

        def freed(eng, name):
            c = CHUNK[name]
            eng.wait_ge(lin_free[c % 2], c // 2 + 1)

        def done(eng, name):
            eng.wait_ge(lin_done, CHUNK[name] + 1)

        def slot(name):
            return lin[CHUNK[name] % 2]

        def free_sem(name):
            return lin_free[CHUNK[name] % 2]

        def shift(n, k):
            return adac[:, 3 * n * KC + k:3 * n * KC + k + 1]

        def col(r):
            return cols[:, r:r + 1]

        ROPED = ["kc", "q0", "q1", "q2", "q3", "ks", "kw"]
        Z = ["kc", "q0", "q1", "q2", "q3", "ks", "vs", "kw", "vw"]
        AUXED = ["kc", "q0", "q1", "q2", "q3", "ks", "vs", "kw", "nsaT", "vw"]

        def clear():
            with nc.Block() as block:
                @block.sync
                def _(sp):
                    for s in every[0::5]:
                        sp.sem_clear(s)

                @block.tensor
                def _(pe):
                    for s in every[1::5]:
                        pe.sem_clear(s)

                @block.scalar
                def _(act):
                    for s in every[2::5]:
                        act.sem_clear(s)

                @block.vector
                def _(dve):
                    for s in every[3::5]:
                        dve.sem_clear(s)

                @block.gpsimd
                def _(pool):
                    for s in every[4::5]:
                        pool.sem_clear(s)

        clear()

        def chunks(s):
            if s["b"] == "w" and s["n"] == 5 * P:
                return [(0, 3 * P, P), (3 * P, 5 * P, 512)]
            return [(c, min(s["n"], c + 512), c) for c in range(0, s["n"], 512)]

        with nc.Fori(0, DEPTH) as layer:
            with nc.Block() as block:
                @block.sync
                def _(sp):
                    def source(t):
                        if t[0] == "split":
                            _, src, row, c0, k, _ = t
                            return a[src][layer, row:row + k * P, c0:c0 + 1024 // k].rearrange("(k p) n -> p k n", p=P)
                        return ada_tile(layer if t[1] >= ADA_FIRST else (layer + 1) % DEPTH, t[1])

                    for n, t in enumerate(TILES):
                        if n == RAW:
                            sp.dma_start(x_keep, xT[:, :, :]).then_inc(x_out, 16)
                        if n >= RAW:
                            o = n - RAW
                            sp.wait_ge(dict(split=w_split, ada=ada_used, cmp=cmp_used)[TILES[o][0]], KIND_NO[o] + 1)
                        if n == TILE_OF[("ua", 4)]:
                            sp.wait_ge(v_done, N_VGROUPS)
                        ready = raw_in[n % RAW]
                        if t[0] == "cmp":
                            src = a["cmp_v_w1" if t[1] else "cmp_k_w1"]
                            for lh in range(2):
                                r0 = (lh * CMP_L // 2 + t[2] * LPT) * HD
                                sp.dma_start(wraw[64 * lh:64 * lh + 64, n % RAW, :].rearrange("p (k n) -> p k n", k=LPT),
                                             src[layer, r0:r0 + LPT * HD, :].rearrange("(k p) n -> p k n", p=HD)
                                             ).then_inc(ready, 16)
                        else:
                            k = t[4] if t[0] == "split" else KC
                            sp.dma_start(wraw[:, n % RAW, :].rearrange("p (k n) -> p k n", k=k), source(t)).then_inc(ready, 16)

                @block.gpsimd
                def _(pool):
                    def attention():
                        for u, here in enumerate(STEPS):
                            for x in here:
                                if x["kind"] != "b":
                                    r = SEEN[x["qt"]] if x["kind"] == "c" else P
                                    pool.wait_ge(t_free[x["bank"]], x["no"] // 2 + 1)
                                    pool.tensor_scalar(pt("high", x, r), pt("both", x, r), 1.0, 1.0, ALU.mult, ALU.mult).then_inc(t_hi, 1)
                                    pool.wait_ge(t_hi, x["v_no"] + 1)
                            for st in SETS:
                                for i in range(HPG):
                                    if st["last"] + SCALED_AFTER[i] == u:
                                        pool.wait_ge(f_made, st["no"] + 1)
                                        p = prob_of(st["no"], i)[:, 0:st["n"]]
                                        pool.tensor_scalar(p, p, fac[:, st["no"] % 2, i:i + 1], 1.0, ALU.mult, ALU.mult).then_inc(p_scaled, 1)
                                        pool.wait_ge(p_scaled, HPG * st["no"] + i + 1)

                    for n, t in enumerate(TILES):
                        if t[0] != "split":
                            continue
                        s = SPLIT_NO[n]
                        if s:
                            pool.wait_ge(w_split, s)
                        if t[5][0] == ("ua", 0):
                            attention()
                            pool.wait_ge(t_done, END_GROUP[len(SETS) - 1]["no"] + 1)
                        pool.wait_ge(raw_in[n % RAW], IN_SLOT[n])
                        if s >= SPL:
                            before = [m for m in SPLIT_NO if SPLIT_NO[m] == s - SPL][0]
                            done(pool, TILES[before][5][-1])
                        pool.tensor_scalar(whi[:, s % SPL, :], wraw[:, n % RAW, :], 1.0, 1.0, ALU.mult, ALU.mult).then_inc(w_hi, 1)
                        pool.wait_ge(w_hi, s + 1)
                        pool.tensor_tensor(wlo[:, s % SPL, :], wraw[:, n % RAW, :], whi[:, s % SPL, :].bitcast(F32),
                                           ALU.subtract).then_inc(w_split, 1)

                @block.tensor
                def _(pe):
                    def dense(name, act_h, act_l, ready=None, beside=None):
                        parts = []
                        for nm in (name, beside)[:1 + (beside is not None)]:
                            c, n = CHUNK[nm], TILE_OF[nm]
                            kk, j = TILES[n][4], TILES[n][5].index(nm)
                            if j == 0:
                                pe.wait_ge(w_split, SPLIT_NO[n] + 1)
                            if c >= 2:
                                pe.wait_ge(lin_free[c % 2], c // 2)
                            parts.append((c, SPLIT_NO[n] % SPL, j))
                        for k in range(kk):
                            if ready:
                                ready(k)
                            for c, s, j in parts:
                                at = k * (1024 // kk) + P * j
                                wh, wl = whi[:, s, at:at + P], wlo[:, s, at:at + P]
                                for w, m in ((wh, act_h), (wh, act_l), (wl, act_h)):
                                    for hf in half:
                                        first = w is wh and m is act_h and k == 0
                                        last = w is wl and k == kk - 1
                                        mm = pe.matmul(lin[c % 2][:, hf], w, m(k)[:, hf], start=first, stop=last)
                                if k == kk - 1:
                                    mm.then_inc(lin_done, 1)

                    ada_no, ada_late = [0], []

                    def ada(j):
                        if ada_late:
                            late = ada_late.pop()
                            ada_column(pe, pv[:, 0, late:late + 1], ada_no[0])
                            ada_no[0] += 1
                        if j is not None:
                            ada_late.append(j)

                    def spread_rms(n):
                        for i, hf in enumerate(half):
                            pe.wait_ge(diag_made, 2 * n + i + 1)
                            pe.matmul(aux[:, hf], ones[:, :], tmp[:, 1, hf], start=True, stop=True).then_inc(spread, 1)

                    def aux_begin(name):
                        i = AUXED.index(name)
                        if i:
                            pe.wait_ge(aux_free, i)

                    def rotate(name):
                        aux_begin(name)
                        pe.wait_ge(z_made, Z.index(name) + 1)
                        for hf in half:
                            mm = pe.matmul(aux[:, hf], rot[:, :], fbuf[:, Z.index(name) % 2, hf], start=True, stop=True)
                        mm.then_inc(aux_done, 1)

                    def token_major(name):
                        aux_begin(name)
                        pe.wait_ge(z_made, Z.index(name) + 1)
                        for t in range(NT):
                            mm = pe.transpose(aux[:, t * P:(t + 1) * P], fbuf[:, Z.index(name) % 2, t * P:(t + 1) * P], ident[:, :])
                        mm.then_inc(aux_done, 1)

                    def compress(kv):
                        pe.wait_ge(blk_made, kv + 1)
                        if kv:
                            pe.wait_ge(cmp_made, 2)
                        for t in range(CMP_T):
                            n = TILE_OF[("cmp", kv, t)]
                            pe.wait_ge(raw_in[n % RAW], IN_SLOT[n])
                            for i in range(LPT):
                                l = t * LPT + i
                                for hc in range(2):
                                    at = i * CMP_H + hc * P
                                    mm = pe.matmul(pv[:, hc, 0:2 * NC], wraw[:, n % RAW, at:at + P], blk[:, l, 0:2 * NC],
                                                   start=l == 0, stop=l == CMP_L // 2 - 1)
                            mm.then_inc(cmp_used, 1)

                    H = lambda k: hH[:, k, :]
                    L = lambda k: hL[:, k, :]

                    pe.transpose(pv[:, 1, 0:P], vecs[:, :], ident[:, :]).then_inc(par_t, 1)
                    spread_rms(0)
                    nxt = iter(range(ADA_FIRST, NADA))
                    for j in range(CONV_W // P):
                        for name in ("cc", "cu", "cb"):
                            if (name, j) == ("cc", 0):
                                dense((name, j), H, L, lambda k: pe.wait_ge(h_lo, k + 1), ("cu", 0))
                            elif (name, j) != ("cu", 0):
                                dense((name, j), H, L)
                            ada(next(nxt))
                    for i in range(0, KC, 2):
                        dense(("gc", i), H, L)
                        ada(next(nxt))
                        dense(("gc", i + 1), H, L)
                        ada(next(nxt))
                        if i == 0:
                            pe.wait_ge(cv_lo, 4)
                        dense(("uc", i), lambda k: cvH[:, k, :], lambda k: cvL[:, k, :])
                        dense(("uc", i + 1), lambda k: cvH[:, k, :], lambda k: cvL[:, k, :])
                        ada(next(nxt))
                    for i in range(KC):
                        dense(("ga", i), H, L)
                        ada(next(nxt))
                    pe.wait_ge(cmp_in, 16 * 6)
                    for i in range(2):
                        mm = pe.transpose(pv[:, 1, P + 32 * i:P + 32 * i + 32], pe_rows[:, i * P:(i + 1) * P],
                                          ident[0:CMP_L, 0:CMP_L])
                    mm.then_inc(par_t, 1)
                    dense("kc", H, L)
                    ada(None)
                    dense("vc", H, L)
                    rotate("kc")
                    dense("q0", H, L)
                    dense("q1", H, L)
                    rotate("q0")
                    pe.wait_ge(ada_cols, 2)
                    compress(0)
                    dense("q2", H, L)
                    rotate("q1")
                    pe.wait_ge(hid_silu, 1)
                    for hc in range(2):
                        mm = pe.matmul(pv[0:HD, 0, 256:256 + 2 * NC], w2[:, 0, hc, :], hsil[:, hc, :], start=hc == 0, stop=hc == 1)
                    mm.then_inc(cmp_done, 1)
                    compress(1)
                    dense("q3", H, L)
                    rotate("q2")
                    pe.wait_ge(hid_silu, 2)
                    for g in range(NKV):
                        for hc in range(2):
                            mm = pe.matmul(pv[0:NC, 0, 256 + g * HD:256 + (g + 1) * HD], hsil[:, hc, g * NC:(g + 1) * NC],
                                           w2[:, 1, hc, :], start=hc == 0, stop=hc == 1)
                    mm.then_inc(cmp_done, 1)
                    dense("ks", H, L)
                    rotate("q3")
                    dense("vs", H, L)
                    rotate("ks")
                    dense("kw", H, L)
                    token_major("vs")
                    dense("ns", H, L)
                    rotate("kw")
                    dense("vw", H, L)
                    aux_begin("nsaT")
                    freed(pe, "ns")
                    for t in range(NT):
                        mm = pe.transpose(aux[:, t * NG:(t + 1) * NG], tmp[0:NG, 1, t * P:(t + 1) * P], ident[0:NG, 0:NG])
                    mm.then_inc(aux_done, 1)
                    token_major("vw")

                    def score(u):
                        s = scores(u)
                        for v in BANK_LAST[u]:
                            if UNITS[v][0] == "c":
                                pe.wait_ge(c_in_made, 1 + NTH[UNITS[v][1]])
                            else:
                                pe.wait_ge(exp_made, SCORES_BEFORE[v + 1])
                        b, qt = UNITS[u][:2]
                        qs = slice(qt * P, (qt + 1) * P)
                        if b == "c":
                            for h in range(NH):
                                mm = pe.matmul(s[:, h * P:h * P + NKV * NC], qS[:, h, qs].bitcast(F32), kcmp[:, :],
                                               start=h % HPG == 0, stop=h % HPG == HPG - 1, skip_group_check=True)
                            mm.then_inc(s_done, 1)
                            return
                        g, i, no = UNITS[u][2:]
                        st = SETS[no]
                        masked = b == "s" and qt >= CHOICE
                        if masked and i == 0 and g == 0:
                            b_ = B_GROUP[qt]
                            pe.wait_ge(t_free[b_["bank"]], b_["no"] // 2 + 1)
                        kh, kl = (kwH, kwL) if b == "w" else (ksH, ksL)
                        for c0, c1, at in chunks(st):
                            k0 = st["lo"] * P + c0
                            q = qS[:, HPG * g + i, qs]
                            wide = max(c1 - c0, 256)
                            mine = []
                            if b == "w" and qt >= WIN_T and c0 == 0:
                                mine.append((at, oldest))
                            if c1 == st["n"]:
                                mine.append((at + c1 - c0 - P, causal))
                            pe.matmul(s[:, at:at + wide], q, kh[:, g, k0:k0 + wide], start=True, stop=False)
                            mm = pe.matmul(s[:, at:at + wide], q, kl[:, g, k0:k0 + wide], start=False, stop=not masked and not mine)
                            if masked:
                                mm = pe.matmul(s[:, at:at + wide], selT[:, qt % 2, g, :], blocks_of[:, k0:k0 + wide],
                                               start=False, stop=not mine)
                            for j, (m0, m) in enumerate(mine):
                                mm = pe.matmul(s[:, m0:m0 + P], identb[:, :], m[:, :], start=False, stop=j == len(mine) - 1)
                        mm.then_inc(s_done, 1)

                    def transpose_group(x):
                        if x["no"] >= 2:
                            pe.wait_ge(t_free[x["bank"]], x["no"] // 2)
                        o = aux[:, x["bank"] * 512:(x["bank"] + 1) * 512]
                        if x["kind"] == "b":
                            pe.wait_ge(sel_made, NTH[x["qt"]] + 1)
                            mm = pe.transpose(o[0:64, 0:P], selb[:, :, :].rearrange("p g n -> p (g n)"), ident[:, :])
                        elif x["kind"] == "c":
                            pe.wait_ge(c_gated, NTH[x["qt"]] + 1)
                            for i in range(HPG):
                                mm = pe.transpose(o[0:SEEN[x["qt"]], i * P:(i + 1) * P], cgated[:, HPG * x["g"] + i, 0:SEEN[x["qt"]]], ident[:, :])
                        else:
                            no = x["set"]["no"]
                            pe.wait_ge(p_scaled, HPG * (no + 1))
                            for i in range(HPG):
                                mm = pe.transpose(o[:, i * P:(i + 1) * P], prob_of(no, i)[:, x["at"]:x["at"] + P], ident[:, :])
                        mm.then_inc(t_done, 1)

                    def values(x):
                        if x["first"] and NTH[x["qt"]]:
                            pe.wait_ge(fin_sum, 2 * (NKV * (NTH[x["qt"]] - 1) + x["g"] + 1))
                        pe.wait_ge(t_lo, x["v_no"] + 1)
                        r = SEEN[x["qt"]] if x["kind"] == "c" else P
                        if x["kind"] == "c":
                            v = vcmp[0:r, x["g"], :]
                        else:
                            v = (vw if x["set"]["b"] == "w" else vs)[:, x["key"], x["g"], :]
                        pe.matmul(pv[:, x["g"], :], v, pt("high", x, r), start=x["first"], stop=False)
                        pe.matmul(pv[:, x["g"], :], v, pt("low", x, r), start=False, stop=x["last"]).then_inc(v_done, 1)

                    pe.wait_ge(rope_made, len(ROPED))
                    pe.wait_ge(cmp_made, 3)
                    freed(pe, "ns")
                    freed(pe, "vw")
                    for u, here in enumerate(STEPS):
                        if u == [bool(x) for x in STEPS].index(True):
                            pe.wait_ge(aux_free, len(AUXED))
                            pe.wait_ge(vc_lo, 1)
                        for v in range(len(UNITS)):
                            if SCORE_STEP[v] == u:
                                score(v)
                        for x in here:
                            transpose_group(x)
                            for v in x["then"]:
                                values(v)
                        for v in FLUSH[u]:
                            values(v)

                    pe.wait_ge(exp_made, SCORES_BEFORE[-1])
                    pe.wait_ge(fin_lo, NKV * NT)
                    for i in range(KC):
                        dense(("ua", i), lambda k: atH[:, k, :], lambda k: atL[:, k, :])
                    for i in range(KC):
                        dense(("wo", i), lambda k: mxH[:, k, :], lambda k: mxL[:, k, :],
                              (lambda k: pe.wait_ge(mg_lo, k + 1)) if i == 0 else None)
                    sum_squares(pe, lambda: pe.wait_ge(ss_added, KC - 2), lambda: pe.wait_ge(sq_made, KC))
                    spread_rms(1)

                    def ff1(fg):
                        for f in range(FG * fg, FG * fg + FG):
                            if f == 0:
                                dense(("f1", f), H, L, lambda k: pe.wait_ge(h_lo, KC + k + 1), ("f1", 1))
                            elif f > 1:
                                dense(("f1", f), H, L)
                            if f < ADA_FIRST:
                                ada(f)
                            elif f == ADA_FIRST:
                                ada(None)

                    ff1(0)
                    for fg in range(NFG):
                        if fg + 1 < NFG:
                            ff1(fg + 1)
                        pe.wait_ge(hid_lo, FG * (fg + 1))
                        for i in range(KC):
                            dense(("f2", fg, i), lambda k: hidH[:, fg % 2, k, :], lambda k: hidL[:, fg % 2, k, :])
                    sum_squares(pe, lambda: pe.wait_ge(ss_added, 2 * (KC - 2)), lambda: pe.wait_ge(sq_made, 2 * KC))

                @block.scalar
                def _(act):
                    def norm(n):
                        act.wait_ge(mean_made, n + 1)
                        act.activation(rms[:, :], rms[:, :], ACT.Sqrt).then_inc(root_made, 1)
                        act.wait_ge(ada_cols, 3 if n else 1)
                        for k in range(KC):
                            act.wait_ge(h_t, n * KC + k + 1)
                            act.activation(hH[:, k, :], nt[:, k % 2, :], ACT.Identity, bias=shift(n, k)).then_inc(h_hi, 1)

                    norm(0)
                    for i, name in enumerate(("cmp_k_pe", "cmp_v_pe")):
                        for j in range(2):
                            act.dma_start(pe_rows[:, i * P + j * HD:i * P + (j + 1) * HD], a[name][layer, :, :]).then_inc(cmp_in, 16)
                    for i, name in enumerate(("cmp_k_w2", "cmp_v_w2")):
                        act.dma_start(w2[:, i, :, :], a[name][layer, :, :].rearrange("(k p) n -> p k n", p=P)).then_inc(cmp_in, 16)
                    act.wait_ge(x_out, 16)
                    act.wait_ge(h_t, KC)
                    for i, t in enumerate((cosT, sinT)):
                        act.dma_start(t[:, :], rope_keep[i]).then_inc(tab_in, 16)
                    for j in range(CONV_W // P):
                        if j:
                            freed(act, ("cu", j - 1))
                        done(act, ("cc", j))
                        act.activation(fbuf[:, 0, :], slot(("cc", j))[:, :], ACT.Identity,
                                       bias=col(R_BIN + O_CC // P + j)).then_inc(free_sem(("cc", j)), 1)
                        act.wait_ge(conv_made, j + 1)
                        act.activation(cvH[:, j, :], ropes[:, 1, :], ACT.Copy).then_inc(cv_hi, 1)
                    for i in range(0, KC, 2):
                        for ii in (i, i + 1):
                            if ii >= 2:
                                freed(act, ("uc", ii - 2))
                            else:
                                act.wait_ge(cv_lo, CONV_W // P)
                            done(act, ("gc", ii))
                            act.activation(fbuf[:, ii % 2, :], slot(("gc", ii))[:, :], ACT.Sigmoid,
                                           bias=col(R_MG + ii)).then_inc(free_sem(("gc", ii)), 1)
                        for ii in (i, i + 1):
                            freed(act, ("uc", ii))
                            act.dma_start(mix_keep[ii], tmp[:, ii % 2, :]).then_inc(mix_out[ii % 2], 16)
                    for i in range(KC):
                        if i >= 2:
                            act.wait_ge(gate_out[i % 2], 16 * (i // 2))
                        done(act, ("ga", i))
                        act.activation(ropes[:, i % 2, :], slot(("ga", i))[:, :], ACT.Sigmoid,
                                       bias=col(R_MG + KC + i)).then_inc(free_sem(("ga", i)), 1)
                        freed(act, ("ga", i))
                        act.dma_start(gate_keep[i], ropes[:, i % 2, :]).then_inc(gate_out[i % 2], 16)
                    for i in range(2):
                        act.wait_ge(mix_out[i], 8 * KC)
                        act.wait_ge(gate_out[i], 8 * KC)

                    def z(name, row, bias=None, scale=1.0):
                        i = Z.index(name)
                        if i >= 2:
                            o = Z[i - 2]
                            if o in ROPED:
                                act.wait_ge(rope_made, ROPED.index(o) + 1)
                            else:
                                act.wait_ge(aux_done, AUXED.index(o) + 1)
                        done(act, name)
                        act.activation(fbuf[:, i % 2, :], slot(name)[:, :], ACT.Identity,
                                       bias=col(row) if bias is None else bias, scale=scale).then_inc(z_made, 1)
                        act.wait_ge(z_made, i + 1)
                        act.sem_inc(free_sem(name), 1)

                    def q(j):
                        z(f"q{j}", 0, qbias[:, j:j + 1], SCALE)

                    def silu(kv):
                        act.wait_ge(cmp_used, CMP_T * (kv + 1))
                        act.activation(hsig[:, :, :], pv[:, :, 0:2 * NC], ACT.Sigmoid).then_inc(hid_sig, 1)

                    def rope_high(name):
                        i = ROPED.index(name)
                        act.wait_ge(rope_sum, i + 1)
                        for g in range(2):
                            rows = slice(HD * g, HD * (g + 1))
                            t = ropes[rows, 0, :]
                            if name[0] == "q":
                                act.activation(qS[rows, 2 * int(name[1]) + g, :], t, ACT.Copy).then_inc(rope_hi, 1)
                            else:
                                kh = ksH if name == "ks" else kwH
                                for r in range(2):
                                    act.activation(kh[HD * r:HD * (r + 1), g, :], t, ACT.Copy).then_inc(rope_hi, 1)

                    def v_high(name, v):
                        act.wait_ge(aux_done, AUXED.index(name) + 1)
                        act.activation(v[:, :, :, 0:HD], aux[:, :].rearrange("p (t g d) -> p t g d", t=NT, g=NKV),
                                       ACT.Copy).then_inc(v_hi, 1)

                    B = lambda o: R_BIN + o // P
                    z("kc", B(O_KC))
                    done(act, "vc")
                    act.activation(vcT[:, :], slot("vc")[:, :], ACT.Identity, bias=col(B(O_VC))).then_inc(free_sem("vc"), 1)
                    q(0)
                    q(1)
                    rope_high("q0")
                    silu(0)
                    q(2)
                    act.wait_ge(cmp_done, 1)
                    for r in range(2):
                        act.activation(kcmp[HD * r:HD * (r + 1), :], pv[0:HD, 0, 256:256 + 2 * NC], ACT.Copy).then_inc(cmp_made, 1)
                    rope_high("q1")
                    silu(1)
                    q(3)
                    rope_high("q2")
                    act.wait_ge(cmp_done, 2)
                    act.activation(vcmp[:, :, 0:HD], pv[0:NC, 0, 256:256 + 2 * HD].rearrange("p (g c) -> p g c", g=NKV),
                                   ACT.Copy).then_inc(cmp_made, 1)
                    z("ks", B(O_KS))
                    rope_high("q3")
                    z("vs", B(O_VS))
                    rope_high("ks")
                    z("kw", B(O_KW))
                    act.wait_ge(blk_made, 2)
                    v_high("vs", vs)
                    done(act, "ns")
                    act.activation(tmp[0:NG, 1, :], slot("ns")[0:NG, :], ACT.Sigmoid, bias=cols[0:NG, R_NSA:R_NSA + 1]
                                   ).then_inc(free_sem("ns"), 1)
                    rope_high("kw")
                    z("vw", B(O_VW))
                    act.wait_ge(rope_sum, len(ROPED))
                    v_high("vw", vw)

                    act.wait_ge(aux_free, len(AUXED))
                    for u, here in enumerate(STEPS):
                        if u < len(UNITS) and UNITS[u][0] == "c":
                            nth, n = NTH[UNITS[u][1]], SEEN[UNITS[u][1]]
                            act.wait_ge(c_in_made, nth + 1)
                            if nth:
                                act.wait_ge(c_gated, nth)
                            act.activation(cprob[:, :, 0:n], scm[:, :, 0:n], ACT.Exp).then_inc(c_exp, 1)
                        elif u < len(UNITS):
                            b, qt, g, i, no = UNITS[u]
                            m, st = SCORES_BEFORE[u], SETS[no]
                            if no >= PROBS and i == 0:
                                act.wait_ge(t_done, END_GROUP[no - PROBS]["no"] + 1)
                            act.wait_ge(max_made, m + 1)
                            at = chunks(st)[0][2]
                            act.activation(prob_of(no, i)[:, 0:st["n"]], scores(u)[:, at:at + st["n"]], ACT.Exp,
                                           bias=negm[:, m:m + 1], accum_out=sums[:, m:m + 1]).then_inc(exp_made, 1)
                        for x in here:
                            o = aux[:, x["bank"] * 512:(x["bank"] + 1) * 512]
                            act.wait_ge(t_done, x["no"] + 1)
                            if x["kind"] == "b":
                                if NTH[x["qt"]] >= 2:
                                    act.wait_ge(s_done, [s for s in SETS if s["qt"] == x["qt"] + 2][-1]["last"] + 1)
                                for g in range(NKV):
                                    ins = act.activation(selT[0:NS, x["qt"] % 2, g, :], o[32 * g:32 * g + NS, 0:P], ACT.Copy)
                                ins.then_inc(t_free[x["bank"]], 1)
                            else:
                                r = SEEN[x["qt"]] if x["kind"] == "c" else P
                                if x["v_no"] >= PT:
                                    act.wait_ge(v_done, x["v_no"] - PT + 1)
                                act.activation(pt("both", x, r), o[0:r, :], ACT.Copy).then_inc(t_free[x["bank"]], 1)
                        for st in SETS:
                            if st["b"] != "s":
                                continue
                            k = NKV * NTH[st["qt"]] + st["g"]
                            if st["fin"] == u:
                                act.wait_ge(v_done, END_GROUP[st["no"]]["v_no"] + 1)
                                if k:
                                    act.wait_ge(fin_sum, 2 * k)
                                act.activation(low_half, pv[HD:P, st["g"], :], ACT.Copy).then_inc(fin_low, 1)
                            if st["fin"] + 2 == u:
                                act.wait_ge(fin_sum, 2 * (k + 1))
                                act.activation(atH[:, 2 * st["g"]:2 * st["g"] + 2, st["qt"] * P:(st["qt"] + 1) * P],
                                               att.rearrange("p (j t) -> p j t", j=2), ACT.Copy).then_inc(o_hi, 1)

                    act.wait_ge(v_done, N_VGROUPS)
                    act.wait_ge(fin_lo, NKV * NT)
                    for i in range(KC + 2):
                        if i < KC:
                            if i >= 2:
                                act.wait_ge(mg_made, i - 1)
                            act.dma_start(stG[:, i % 2, :], gate_keep[i]).then_inc(fetch_sem[i % 2], 16)
                            act.dma_start(stM[:, i % 2, :], mix_keep[i]).then_inc(fetch_sem[i % 2], 16)
                            act.dma_start(xT[:, i, :], x_keep[:, i, :]).then_inc(x_back, 16)
                        if i >= 2:
                            act.wait_ge(mg_made, i - 1)
                            act.activation(mxH[:, i - 2, :], tmp[:, i % 2, :], ACT.Copy).then_inc(mg_hi, 1)

                    def squares(i, n):
                        act.wait_ge(x_made, (NFG - 1) * KC * n + n * KC + i + 1)
                        if i >= 2:
                            act.wait_ge(ss_added, n * (KC - 2) + i - 1)
                        act.activation(tmp[:, min(i, 1), :], xT[:, i, :], ACT.Square).then_inc(sq_made, 1)

                    act.wait_ge(mg_lo, KC)
                    for i in range(KC):
                        squares(i, 0)
                    norm(1)

                    def ff1(fg):
                        for f in range(FG * fg, FG * fg + FG):
                            done(act, ("f1", f))
                            if f:
                                act.wait_ge(hid_sq, f)
                                act.wait_ge(hid_hi, f)
                            else:
                                act.wait_ge(h_lo, 2 * KC)
                            act.activation(tmp[:, 0, :], slot(("f1", f))[:, :], ACT.Relu).then_inc(relu_made, 1)
                            act.wait_ge(relu_made, f + 1)
                            act.sem_inc(free_sem(("f1", f)), 1)
                            if fg >= 2:
                                done(act, ("f2", fg - 2, KC - 1))
                            act.activation(hidH[:, fg % 2, f % FG, :], tmp[:, 0, :], ACT.Square).then_inc(hid_hi, 1)

                    act.wait_ge(par_t, 1)
                    load_vectors(act, (layer + 1) % DEPTH)
                    for fg in range(NFG):
                        ff1(fg)
                    act.wait_ge(par_in, 16 * N_ROWS)
                    act.wait_ge(hid_lo, NFG * FG)
                    for i in range(KC):
                        squares(i, 1)

                @block.vector
                def _(dve):
                    n_then = [0]

                    def then(ins):
                        n_then[0] += 1
                        ins.then_inc(dve_step, 1)
                        dve.wait_ge(dve_step, n_then[0])

                    def mod(n):
                        sc = adac[:, (3 * n + 1) * KC:(3 * n + 2) * KC]
                        g = cols[:, (R_GMLP if n else R_GMIX):(R_GMLP if n else R_GMIX) + KC]
                        return dve.scalar_tensor_tensor(out=modA[:, n, :], in0=sc, scalar=1.0, in1=g, op0=ALU.add, op1=ALU.mult)

                    def ada_part(lo, hi):
                        then(dve.tensor_tensor(adac[:, lo:hi], pv[:, 0, lo:hi], cols[:, R_ADA + lo:R_ADA + hi], ALU.add))

                    ada_tiles = iter([n for n, t in enumerate(TILES) if t[0] == "ada"])

                    def ada():
                        n = next(ada_tiles)
                        ada_products(dve, n, KIND_NO[n], IN_SLOT[n])

                    def norm(n):
                        if n:
                            dve.wait_ge(ss_done, 1)
                        dve.tensor_scalar(rms[:, :], aux[:, 0:NT], 1.0 / D, EPS, ALU.mult, ALU.add).then_inc(mean_made, 1)
                        dve.wait_ge(root_made, n + 1)
                        dve.reciprocal(rms[:, :], rms[:, :]).then_inc(rstd_made, 1)
                        dve.wait_ge(rstd_made, n + 1)
                        for i in range(2):
                            ti = slice(4 * i, 4 * i + 4)
                            dve.tensor_tensor(tmp[:, 1, half[i]].rearrange("p (t c) -> p t c", t=4),
                                              ident[:, :].rearrange("p (o c) -> p o c", o=1).to_broadcast([P, 4, P]),
                                              rms[:, ti].rearrange("p (t o) -> p t o", o=1).to_broadcast([P, 4, P]),
                                              ALU.mult).then_inc(diag_made, 1)
                        if n == 0:
                            dve.wait_ge(par_t, 1)
                            then(dve.tensor_copy(cols[:, :], pv[:, 1, 0:P]))
                            qr = R_BIN + O_Q // P
                            then(dve.tensor_scalar(qbias[:, :], cols[:, qr:qr + 4], SCALE, None, ALU.mult))
                            then(dve.tensor_tensor(adac[:, 0:ADA_FIRST], adac[:, 0:ADA_FIRST], cols[:, R_ADA:R_ADA + ADA_FIRST], ALU.add))
                            mod(0).then_inc(ada_cols, 1)
                            dve.wait_ge(ada_cols, 1)
                        dve.wait_ge(spread, 2 * (n + 1))

                        def low(k):
                            dve.wait_ge(h_hi, n * KC + k + 1)
                            dve.scalar_tensor_tensor(out=hL[:, k, :], in0=nt[:, k % 2, :], scalar=shift(n, k), in1=hH[:, k, :].bitcast(F32),
                                                     op0=ALU.add, op1=ALU.subtract).then_inc(h_lo, 1)

                        if n:
                            dve.wait_ge(ada_cols, 3)
                        for k in range(KC):
                            m = n * KC + k
                            if k >= 2:
                                dve.wait_ge(h_lo, m - 1)
                            dve.scalar_tensor_tensor(out=nt[:, k % 2, :], in0=xT[:, k, :], scalar=modA[:, n, k:k + 1], in1=aux[:, :],
                                                     op0=ALU.mult, op1=ALU.mult).then_inc(h_t, 1)
                            if k:
                                low(k - 1)
                        low(KC - 1)

                    norm(0)
                    v, y, cf = fbuf[:, 1, :], ropes[:, 0, :], ropes[:, 1, :]
                    dve.wait_ge(x_out, 16)
                    for j in range(CONV_W // P):
                        ada()
                        ada()
                        freed(dve, ("cc", j))
                        done(dve, ("cu", j))
                        dve.scalar_tensor_tensor(out=v, in0=slot(("cu", j))[:, :], scalar=col(R_BIN + O_CU // P + j), in1=fbuf[:, 0, :],
                                                 op0=ALU.add, op1=ALU.mult).then_inc(free_sem(("cu", j)), 1)
                        freed(dve, ("cu", j))
                        w = [col(R_CONV + k * (CONV_W // P) + j) for k in range(CONV_K)]
                        then(dve.tensor_scalar(y, v, w[2], None, ALU.mult))
                        then(dve.scalar_tensor_tensor(out=y[:, 1:SEQ], in0=v[:, 0:SEQ - 1], scalar=w[1], in1=y[:, 1:SEQ], op0=ALU.mult, op1=ALU.add))
                        then(dve.scalar_tensor_tensor(out=y[:, 2:SEQ], in0=v[:, 0:SEQ - 2], scalar=w[0], in1=y[:, 2:SEQ], op0=ALU.mult, op1=ALU.add))
                        ada()
                        done(dve, ("cb", j))
                        dve.scalar_tensor_tensor(out=cf, in0=slot(("cb", j))[:, :], scalar=col(R_BIN + O_CB // P + j), in1=y,
                                                 op0=ALU.add, op1=ALU.mult).then_inc(conv_made, 1)
                        dve.wait_ge(conv_made, j + 1)
                        dve.sem_inc(free_sem(("cb", j)), 1)
                        dve.wait_ge(cv_hi, j + 1)
                        dve.tensor_tensor(cvL[:, j, :], cf, cvH[:, j, :].bitcast(F32), ALU.subtract).then_inc(cv_lo, 1)
                    dve.wait_ge(h_lo, KC)
                    for i in range(KC):
                        if i % 2 == 0:
                            ada()
                            ada()
                        freed(dve, ("gc", i))
                        done(dve, ("uc", i))
                        if i >= 2:
                            dve.wait_ge(mix_out[i % 2], 16 * (i // 2))
                        dve.tensor_tensor(tmp[:, i % 2, :], slot(("uc", i))[:, :], fbuf[:, i % 2, :], ALU.mult).then_inc(free_sem(("uc", i)), 1)
                        if i % 2:
                            ada()
                    for i in range(KC):
                        ada()
                    dve.wait_ge(ada_mm, NADA - ADA_FIRST)
                    ada_part(ADA_FIRST, NADA)
                    dve.sem_inc(ada_cols, 1)
                    mod(1).then_inc(ada_cols, 1)

                    def rope(name):
                        i = ROPED.index(name)
                        f, t1, t2 = fbuf[:, Z.index(name) % 2, :], ropes[:, 0, :], ropes[:, 1, :]
                        dve.wait_ge(z_made, Z.index(name) + 1)
                        if i:
                            dve.wait_ge(rope_made, i)
                        dve.tensor_tensor(t2, f, cosT[:, :], ALU.mult).then_inc(dve_step, 1)
                        n_then[0] += 1
                        dve.wait_ge(aux_done, AUXED.index(name) + 1)
                        dve.tensor_tensor(t1, aux[:, :], sinT[:, :], ALU.mult).then_inc(aux_free, 1)
                        dve.wait_ge(aux_free, AUXED.index(name) + 1)
                        dve.wait_ge(dve_step, n_then[0])
                        if name == "kc":
                            dve.tensor_tensor(kcT[:, :], t1, t2, ALU.add).then_inc(rope_made, 1)
                            dve.sem_inc(rope_sum, 1)
                            return
                        dve.tensor_tensor(t1, t1, t2, ALU.add).then_inc(rope_sum, 1)
                        dve.wait_ge(rope_sum, i + 1)
                        dve.wait_ge(rope_hi, 2 * min(i, 4) + 4 * max(0, i - 4))
                        for g in range(2):
                            rows = slice(HD * g, HD * (g + 1))
                            if name[0] == "q":
                                h = 2 * int(name[1]) + g
                                ins = dve.tensor_tensor(qS[HD * (1 - g):HD * (2 - g), h, :], t1[rows], qS[rows, h, :].bitcast(F32), ALU.subtract)
                            else:
                                kh, kl = (ksH, ksL) if name == "ks" else (kwH, kwL)
                                for r in range(2):
                                    ins = dve.tensor_tensor(kl[HD * r:HD * (r + 1), g, :], t1[rows], kh[rows, g, :].bitcast(F32), ALU.subtract)
                        ins.then_inc(rope_made, 1)

                    def v_low(name, v):
                        dve.wait_ge(v_hi, 1 + (name == "vw"))
                        dve.tensor_tensor(v[:, :, :, HD:P], aux[:, :].rearrange("p (t g d) -> p t g d", t=NT, g=NKV),
                                          v[:, :, :, 0:HD].bitcast(F32), ALU.subtract).then_inc(aux_free, 1)

                    def blocks(kv):
                        src = vcT if kv else kcT
                        for g in range(NKV):
                            for lh in range(2):
                                i0 = src[HD * g:HD * (g + 1), CMP_D * lh:CMP_D * (lh + NC)].rearrange("p (c l) -> p l c", l=CMP_D)
                                i1 = pe_cols[HD * g:HD * (g + 1), kv, lh * CMP_D:(lh + 1) * CMP_D].rearrange(
                                    "p (l o) -> p l o", o=1).to_broadcast([HD, CMP_D, NC])
                                ins = dve.tensor_tensor(blk[HD * lh:HD * (lh + 1), :, g * NC:(g + 1) * NC], i0, i1, ALU.add)
                        ins.then_inc(blk_made, 1)

                    def silu(kv):
                        dve.wait_ge(hid_sig, kv + 1)
                        dve.tensor_tensor(hsil[:, :, :], hsig[:, :, :], pv[:, :, 0:2 * NC], ALU.mult).then_inc(hid_silu, 1)

                    dve.wait_ge(par_t, 2)
                    then(dve.tensor_copy(pe_cols[:, :, :].rearrange("p i l -> p (i l)"), pv[:, 1, P:P + 2 * CMP_L]))
                    dve.wait_ge(tab_in, 32)
                    for i in range(2):
                        dve.wait_ge(gate_out[i], 8 * KC)
                    rope("kc")
                    dve.wait_ge(rope_made, 1)
                    blocks(0)
                    rope("q0")
                    silu(0)
                    freed(dve, "vc")
                    blocks(1)
                    rope("q1")
                    silu(1)
                    rope("q2")
                    dve.wait_ge(cmp_made, 3)
                    dve.tensor_tensor(vcmp[:, :, HD:P], pv[0:NC, 0, 256:256 + 2 * HD].rearrange("p (g c) -> p g c", g=NKV),
                                      vcmp[:, :, 0:HD].bitcast(F32), ALU.subtract).then_inc(vc_lo, 1)
                    rope("q3")
                    rope("ks")
                    v_low("vs", vs)
                    rope("kw")
                    dve.wait_ge(aux_done, AUXED.index("nsaT") + 1)
                    dve.tensor_copy(gates[:, :, :].rearrange("p t n -> p (t n)"), aux[:, 0:NT * NG]).then_inc(aux_free, 1)
                    v_low("vw", vw)

                    dve.wait_ge(aux_free, len(AUXED))
                    dve.wait_ge(rope_made, len(ROPED))

                    def bc(t, n):
                        return t.rearrange("p (h o) -> p h o", o=1).to_broadcast([P, t.shape[1], n])

                    then(dve.memset(selb[:, :, :], 0.0))
                    mx8, sum8, r8 = (cst[:, i, :] for i in range(3))
                    def cmp_scores(u, qt):
                        n = SEEN[qt]
                        m = cmask[:, 56 - 8 * qt:56 - 8 * qt + n].rearrange("p (o c) -> p o c", o=1).to_broadcast([P, HPG, n])
                        if NTH[qt]:
                            dve.wait_ge(c_exp, NTH[qt])
                        for g in range(NKV):
                            s3 = scores(u)[:, g * 512:(g + 1) * 512].rearrange("p (h c) -> p h c", h=HPG)[:, :, g * NC:g * NC + n]
                            ins = dve.tensor_tensor(scm[:, HPG * g:HPG * (g + 1), 0:n], s3, m, ALU.add)
                        then(ins)
                        then(dve.tensor_reduce(mx8, scm[:, :, 0:n], AX.X, ALU.max))
                        dve.tensor_tensor(scm[:, :, 0:n], scm[:, :, 0:n], bc(mx8, n), ALU.subtract).then_inc(c_in_made, 1)

                    def cmp_probs(qt):
                        n = SEEN[qt]
                        c3 = cprob[:, :, 0:n]
                        dve.wait_ge(c_exp, NTH[qt] + 1)
                        then(dve.tensor_reduce(sum8, c3, AX.X, ALU.add))
                        then(dve.reciprocal(r8, sum8))
                        if qt == 0:
                            then(dve.tensor_scalar(r8, r8, rowok[:, 0:1], None, ALU.mult))
                        gate = gates[:, qt, 0:NH]
                        if qt < CHOICE:
                            then(dve.tensor_tensor(r8, r8, gate, ALU.mult))
                            gate = r8
                        else:
                            then(dve.tensor_tensor(c3, c3, bc(r8, n), ALU.mult))
                        if NTH[qt]:
                            dve.wait_ge(t_done, C_GROUP[qt + 1, NKV - 1]["no"] + 1)
                        dve.tensor_tensor(cgated[:, :, 0:n], c3, bc(gate, n), ALU.mult).then_inc(c_gated, 1)
                        if qt < CHOICE:
                            return
                        then(dve.memset(psum4[:, :, :], 0.0))
                        p4 = cprob.rearrange("p (g i) c -> p g c i", g=NKV)[:, :, 0:n, :]
                        then(dve.tensor_reduce(psum4[:, :, 1:1 + n], p4, AX.X, ALU.add))

                    def select(qt):
                        q4 = psum4[:, :, 1:65].rearrange("p g (n i) -> p g n i", i=4)
                        then(dve.tensor_reduce(imp[:, :, :], q4, AX.X, ALU.add))
                        before = psum4[:, :, 0:64].rearrange("p g (n i) -> p g n i", i=4)[:, :, :, 0]
                        then(dve.tensor_tensor(imp[:, :, :], imp[:, :, :], before, ALU.add))
                        for tab, op in ((vtab, ALU.mult), (ftab, ALU.add)):
                            tb = tab[:, 14 - 2 * qt:14 - 2 * qt + NS].rearrange("p (o n) -> p o n", o=1).to_broadcast([P, NKV, NS])
                            then(dve.tensor_tensor(imp[:, :, :], imp[:, :, :], tb, op))
                        then(dve.memset(imp[:, :, 0:1], 2 * BONUS))
                        for g in range(NKV):
                            ins = dve.max(top8[:, g, :], imp[:, g, :])
                        then(ins)
                        for g in range(NKV):
                            ins = dve.match_replace(left[:, g, :], top8[:, g, :], imp[:, g, :], TAKEN)
                        then(ins)
                        if NTH[qt]:
                            dve.wait_ge(t_done, B_GROUP[qt + 1]["no"] + 1)
                        dve.tensor_scalar(selb[:, :, 0:NS], left[:, :, :], TAKEN / 10, NEG, ALU.is_lt, ALU.mult).then_inc(sel_made, 1)

                    def factors(st):
                        no, m = st["no"], SCORES_BEFORE[st["first"]]
                        f = fac[:, no % 2, :]
                        dve.wait_ge(exp_made, m + HPG)
                        if no >= 2:
                            dve.wait_ge(p_scaled, HPG * (no - 1))
                        then(dve.reciprocal(f, sums[:, m:m + HPG]))
                        gt = BRANCH[st["b"]] * NH + HPG * st["g"]
                        dve.tensor_tensor(f, f, gates[:, st["qt"], gt:gt + HPG], ALU.mult).then_inc(f_made, 1)

                    for u in range(len(STEPS)):
                        if u < len(UNITS):
                            dve.wait_ge(s_done, u + 1)
                            if UNITS[u][0] == "c":
                                cmp_scores(u, UNITS[u][1])
                            else:
                                st, m = SETS[UNITS[u][4]], SCORES_BEFORE[u]
                                at = chunks(st)[0][2]
                                dve.tensor_reduce(negm[:, m:m + 1], scores(u)[:, at:at + st["n"]], AX.X, ALU.max, negate=True).then_inc(max_made, 1)
                        for x in STEPS[u - 1] if u else []:
                            if x["kind"] != "b":
                                r = SEEN[x["qt"]] if x["kind"] == "c" else P
                                dve.wait_ge(t_hi, x["v_no"] + 1)
                                dve.tensor_tensor(pt("low", x, r), pt("both", x, r), pt("high", x, r).bitcast(F32),
                                                  ALU.subtract).then_inc(t_lo, 1)
                        for st in SETS:
                            if st["last"] + 1 == u:
                                factors(st)
                        if 1 <= u <= len(UNITS) and UNITS[u - 1][0] == "c":
                            cmp_probs(UNITS[u - 1][1])
                        if 2 <= u < len(UNITS) + 2 and UNITS[u - 2][0] == "c" and UNITS[u - 2][1] >= CHOICE:
                            select(UNITS[u - 2][1])
                        for st in SETS:
                            if st["b"] != "s":
                                continue
                            k = NKV * NTH[st["qt"]] + st["g"]
                            if st["fin"] + 1 == u:
                                dve.wait_ge(fin_low, k + 1)
                                if k:
                                    dve.wait_ge(fin_lo, k)
                                for odd in range(2):
                                    pick = lambda t: t.rearrange("p (j o t) -> p j o t", j=2, o=2)[:, :, odd, :]
                                    dve.tensor_tensor(att[HD * odd:HD * (odd + 1), :].rearrange("p (j t) -> p j t", j=2),
                                                      pick(pv[0:HD, st["g"], :]), pick(low_half), ALU.add).then_inc(fin_sum, 1)
                            if st["fin"] + 3 == u:
                                dve.wait_ge(o_hi, k + 1)
                                at_ = (slice(None), slice(2 * st["g"], 2 * st["g"] + 2), slice(st["qt"] * P, (st["qt"] + 1) * P))
                                dve.tensor_tensor(atL[at_], att.rearrange("p (j t) -> p j t", j=2), atH[at_].bitcast(F32),
                                                  ALU.subtract).then_inc(fin_lo, 1)

                    for i in range(KC + 1):
                        if i < KC:
                            t = tmp[:, i % 2, :]
                            done(dve, ("ua", i))
                            dve.wait_ge(fetch_sem[i % 2], 32 * (i // 2 + 1))
                            if i >= 2:
                                dve.wait_ge(mg_lo, i - 1)
                            dve.tensor_tensor(t, slot(("ua", i))[:, :], stG[:, i % 2, :], ALU.mult).then_inc(free_sem(("ua", i)), 1)
                            freed(dve, ("ua", i))
                            dve.tensor_tensor(t, t, stM[:, i % 2, :], ALU.add).then_inc(mg_made, 1)
                        if i:
                            dve.wait_ge(mg_hi, i)
                            dve.tensor_tensor(mxL[:, i - 1, :], tmp[:, (i - 1) % 2, :], mxH[:, i - 1, :].bitcast(F32),
                                              ALU.subtract).then_inc(mg_lo, 1)

                    def add_squares(i, n):
                        if 0 < i < KC - 1:
                            dve.wait_ge(sq_made, n * KC + i + 1)
                            dve.tensor_tensor(tmp[:, 0, :], tmp[:, 0, :], tmp[:, 1, :], ALU.add).then_inc(ss_added, 1)
                            dve.wait_ge(ss_added, n * (KC - 2) + i)

                    n_x = [0]

                    def residual(name, gate, i):
                        done(dve, name)
                        dve.scalar_tensor_tensor(out=xT[:, i, :], in0=slot(name)[:, :], scalar=adac[:, gate + i:gate + i + 1],
                                                 in1=xT[:, i, :], op0=ALU.mult, op1=ALU.add).then_inc(x_made, 1)
                        n_x[0] += 1
                        dve.wait_ge(x_made, n_x[0])
                        dve.sem_inc(free_sem(name), 1)

                    dve.wait_ge(x_back, 16 * KC)
                    for i in range(KC):
                        add_squares(i - 1, 0)
                        residual(("wo", i), 2 * KC, i)
                    norm(1)

                    def ff1(fg):
                        for f in range(FG * fg, FG * fg + FG):
                            if f < ADA_FIRST:
                                ada()
                            dve.wait_ge(relu_made, f + 1)
                            if f:
                                dve.wait_ge(hid_lo, f)
                            dve.tensor_tensor(tmp[:, 1, :], tmp[:, 0, :], tmp[:, 0, :], ALU.mult).then_inc(hid_sq, 1)
                            dve.wait_ge(hid_sq, f + 1)
                            dve.wait_ge(hid_hi, f + 1)
                            dve.tensor_tensor(hidL[:, fg % 2, f % FG, :], tmp[:, 1, :], hidH[:, fg % 2, f % FG, :].bitcast(F32),
                                              ALU.subtract).then_inc(hid_lo, 1)

                    ff1(0)
                    for fg in range(NFG):
                        if fg + 1 < NFG:
                            ff1(fg + 1)
                        for i in range(KC):
                            if fg == NFG - 1:
                                add_squares(i - 1, 1)
                            residual(("f2", fg, i), 5 * KC, i)
                    dve.wait_ge(ada_mm, NADA)
                    dve.tensor_copy(adac[:, 0:ADA_FIRST], pv[:, 0, 0:ADA_FIRST])

            clear()

        f_v, f_a, f_tr, f_out = sem("f_v"), sem("f_a"), sem("f_tr"), sem("f_out")
        f_free = [sem(f"f_free{i}") for i in range(2)]
        g_fin = lambda k: cols[:, R_GFIN + k:R_GFIN + k + 1]
        ON_DVE = (0, 1, 4, 5)
        with nc.Block() as block:
            @block.tensor
            def _(pe):
                for g in range(2 * NT):
                    t, hh = g // 2, g % 2
                    if g < 2:
                        pe.wait_ge(f_v, 2 * (hh + 1))
                        pe.wait_ge(f_a, 2 * (hh + 1))
                    if g >= 4:
                        pe.wait_ge(f_free[hh], t - 1)
                    for i in range(4):
                        at = hh * 512 + i * P
                        mm = pe.transpose(lin[t % 2][:, at:at + P], xT[:, 4 * hh + i, t * P:(t + 1) * P], ident[:, :])
                    mm.then_inc(f_tr, 1)

            @block.scalar
            def _(act):
                for k in range(KC):
                    if k not in ON_DVE:
                        act.activation(xT[:, k, :], xT[:, k, :], ACT.Copy, scale=g_fin(k)).then_inc(f_a, 1)
                act.wait_ge(mean_made, 1)
                act.activation(rms[:, :], rms[:, :], ACT.Sqrt).then_inc(root_made, 1)
                act.wait_ge(rstd_made, 1)
                for t in range(NT):
                    act.wait_ge(f_tr, 2 * t + 2)
                    act.activation(outb[:, t, half[1]], lin[t % 2][:, half[1]], ACT.Copy, scale=rms[:, t:t + 1]).then_inc(f_free[1], 1)

            @block.vector
            def _(dve):
                for k in ON_DVE:
                    dve.tensor_scalar(xT[:, k, :], xT[:, k, :], g_fin(k), None, ALU.mult).then_inc(f_v, 1)
                dve.tensor_scalar(rms[:, :], aux[:, 0:NT], 1.0 / D, EPS, ALU.mult, ALU.add).then_inc(mean_made, 1)
                dve.wait_ge(root_made, 1)
                dve.reciprocal(rms[:, :], rms[:, :]).then_inc(rstd_made, 1)
                dve.wait_ge(rstd_made, 1)
                for t in range(NT):
                    dve.wait_ge(f_tr, 2 * t + 1)
                    dve.tensor_scalar(outb[:, t, half[0]], lin[t % 2][:, half[0]], rms[:, t:t + 1], None, ALU.mult).then_inc(f_free[0], 1)

            @block.sync
            def _(sp):
                for t in range(NT):
                    for hh in range(2):
                        sp.wait_ge(f_free[hh], t + 1)
                    sp.dma_start(out[0, t * P:(t + 1) * P, :], outb[:, t, :]).then_inc(f_out, 16)
                sp.wait_ge(f_out, 16 * NT)


_INS = ["x", "c", "positions", "w_ada", "b_ada", "g_mix", "w_in", "b_in", "conv_w", "cmp_k_w1", "cmp_k_w2", "cmp_k_pe",
        "cmp_v_w1", "cmp_v_w2", "cmp_v_pe", "w_up_conv", "w_up_attn", "w_o", "g_mlp", "w_ff1", "w_ff2", "g_final"]


def kernel(**inputs):
    import concourse.bacc as _bacc
    from concourse.bass_utils import run_bass_kernel_spmd as _run

    nc = _bacc.Bacc("TRN2", target_bir_lowering=False, num_devices=1)
    arrays, aps = {}, {}
    for name in _INS:
        arr = np.ascontiguousarray(inputs[name])
        arrays[f"in_{name}"] = arr
        aps[name] = nc.dram_tensor(f"in_{name}", arr.shape, mybir.dt.from_np(arr.dtype), kind="ExternalInput").ap()
    out = nc.dram_tensor("out_x", (1, SEQ, D), F32, kind="ExternalOutput").ap()
    trunk(nc, aps, out)
    r = _run(nc, [arrays], core_ids=[0])
    return r.results[0]["out_x"]
```
